# Optimizing a Trainium2 kernel written in Bass

```python
import math
import jax, jax.numpy as jnp
from jax import lax
import numpy as np

D_MODEL = 1024
BATCH = 1
SEQ = 512
DEPTH = 2

GRID_W = 64
CTX_LEN = 256
HEAD_DIM = 64
GQA_Q_HEADS = 8
GQA_KV_HEADS = 2
GQA_GROUP = GQA_Q_HEADS // GQA_KV_HEADS
DIFF_HEADS = 4
DIFF_V_DIM = 2 * HEAD_DIM
CONV_CH = 512
CONV_WIDTH = 31
D_FF = -(-8 * D_MODEL // (3 * 256)) * 256
Q_BLOCK = 128
ROPE_THETA = 10000.0
EPS = 1e-6
ATTN_SCALE = HEAD_DIM ** -0.5

GQA_Q_W = GQA_Q_HEADS * HEAD_DIM
GQA_KV_W = GQA_KV_HEADS * HEAD_DIM
DIFF_QK_W = DIFF_HEADS * 2 * HEAD_DIM
DIFF_V_W = DIFF_HEADS * DIFF_V_DIM
CONV_IN_W = 2 * CONV_CH
IN_WIDTHS = (GQA_Q_W, GQA_KV_W, GQA_KV_W, DIFF_QK_W, DIFF_QK_W, DIFF_V_W, CONV_IN_W)
D_IN = sum(IN_WIDTHS)
IN_OFFSETS = tuple(int(v) for v in np.cumsum(IN_WIDTHS)[:-1])
N_BRANCH = 3

kernel_name = "hybrid_gqa_diffattn_conformer_prefix_dit"

def rms_norm(x, g):
    xf = x.astype(jnp.float32)
    y = xf * lax.rsqrt(jnp.mean(xf * xf, axis=-1, keepdims=True) + EPS)
    return (y * g.astype(jnp.float32)).astype(x.dtype)

def layer_norm(x, g, b):
    xf = x.astype(jnp.float32)
    mu = jnp.mean(xf, axis=-1, keepdims=True)
    xc = xf - mu
    var = jnp.mean(xc * xc, axis=-1, keepdims=True)
    y = xc * lax.rsqrt(var + EPS) * g.astype(jnp.float32) + b.astype(jnp.float32)
    return y.astype(x.dtype)

def modulate(h, shift, scale):
    return h * (1 + scale) + shift

def axial_rope_tables(n_tokens):
    rows = n_tokens // GRID_W
    row = jnp.repeat(jnp.arange(rows, dtype=jnp.float32), GRID_W)
    col = jnp.tile(jnp.arange(GRID_W, dtype=jnp.float32), rows)
    n_freq = HEAD_DIM // 4
    inv = ROPE_THETA ** (-jnp.arange(n_freq, dtype=jnp.float32) / n_freq)
    ang = jnp.stack([row[:, None] * inv, col[:, None] * inv], axis=1)
    return jnp.cos(ang), jnp.sin(ang)

def apply_axial_rope(x, cos, sin):
    n_freq = HEAD_DIM // 4
    mid = (1,) * (x.ndim - 3)
    cb = cos.reshape((cos.shape[0],) + mid + (2, n_freq))
    sb = sin.reshape((sin.shape[0],) + mid + (2, n_freq))
    xf = x.astype(jnp.float32).reshape(x.shape[:-1] + (2, 2, n_freq))
    x1 = xf[..., 0, :]
    x2 = xf[..., 1, :]
    out = jnp.stack([x1 * cb - x2 * sb, x2 * cb + x1 * sb], axis=-2)
    return out.reshape(x.shape).astype(x.dtype)

def project_heads(p, g_q_gqa, g_k_gqa, g_q_diff, g_k_diff, rope):
    B, T, _ = p.shape
    gq, gk, gv, dq, dk, dv, cu = jnp.split(p, IN_OFFSETS, axis=-1)
    gq = rms_norm(gq.reshape(B, T, GQA_KV_HEADS, GQA_GROUP, HEAD_DIM), g_q_gqa)
    gk = rms_norm(gk.reshape(B, T, GQA_KV_HEADS, HEAD_DIM), g_k_gqa)
    gv = gv.reshape(B, T, GQA_KV_HEADS, HEAD_DIM)
    dq = rms_norm(dq.reshape(B, T, DIFF_HEADS, 2, HEAD_DIM), g_q_diff)
    dk = rms_norm(dk.reshape(B, T, DIFF_HEADS, 2, HEAD_DIM), g_k_diff)
    dv = dv.reshape(B, T, DIFF_HEADS, DIFF_V_DIM)
    if rope is not None:
        cos, sin = rope
        gq = apply_axial_rope(gq, cos, sin)
        gk = apply_axial_rope(gk, cos, sin)
        dq = apply_axial_rope(dq, cos, sin)
        dk = apply_axial_rope(dk, cos, sin)
    return gq, gk, gv, dq, dk, dv, cu

def gqa_attend(q, k, v):
    s = jnp.einsum('bqkgd,btkd->bkgqt', q * ATTN_SCALE, k).astype(jnp.float32)
    p = jax.nn.softmax(s, axis=-1).astype(v.dtype)
    return jnp.einsum('bkgqt,btkd->bqkgd', p, v)

def diff_attend(q, k, v, lam):
    s = jnp.einsum('bqhmd,bthmd->bhmqt', q * ATTN_SCALE, k).astype(jnp.float32)
    p = jax.nn.softmax(s, axis=-1)
    w = (p[:, :, 0] - lam * p[:, :, 1]).astype(v.dtype)
    return jnp.einsum('bhqt,bthe->bqhe', w, v)

def blocked_queries(fn, q):
    B, T = q.shape[:2]
    nb = T // Q_BLOCK
    qb = jnp.moveaxis(q.reshape((B, nb, Q_BLOCK) + q.shape[2:]), 1, 0)
    ob = lax.map(fn, qb)
    return jnp.moveaxis(ob, 0, 1).reshape((B, T) + ob.shape[3:])

def depthwise_conv(u, w, b):
    out = lax.conv_general_dilated(
        u, w[:, None, :].astype(u.dtype), window_strides=(1,),
        padding=[(CONV_WIDTH // 2, CONV_WIDTH // 2)],
        dimension_numbers=('NWC', 'WIO', 'NWC'),
        feature_group_count=u.shape[-1])
    return out + b

def conformer_conv(cu, w_dw, b_dw, g_ln, b_ln, w_c):
    a, g = jnp.split(cu, 2, axis=-1)
    u = a * jax.nn.sigmoid(g)
    u = depthwise_conv(u, w_dw, b_dw)
    u = jax.nn.silu(layer_norm(u, g_ln, b_ln))
    return u @ w_c

def merge_branches(h, o_gqa, o_diff, cu, lam_init, g_subln, w_a, w_b, w_dw, b_dw, g_ln, b_ln, w_c,
                   w_gate, b_gate, w_out):
    B, T, _ = h.shape
    y_a = o_gqa.reshape(B, T, GQA_Q_W) @ w_a
    o_diff = rms_norm(o_diff, g_subln) * (1.0 - lam_init)
    y_b = o_diff.reshape(B, T, DIFF_V_W) @ w_b
    y_c = conformer_conv(cu, w_dw, b_dw, g_ln, b_ln, w_c)
    gates = jax.nn.sigmoid(h @ w_gate + b_gate)
    g_a, g_b, g_c = jnp.split(gates, N_BRANCH, axis=-1)
    return (g_a * y_a + g_b * y_b + g_c * y_c) @ w_out

def swiglu(h, w_in, w_out):
    g, u = jnp.split(h @ w_in, 2, axis=-1)
    return (jax.nn.silu(g) * u) @ w_out

def setup_inputs(seed: int = 0) -> dict:
    key = jax.random.key(seed)
    ks = jax.random.split(key, 32)
    f32 = jnp.float32
    nrm = lambda k, shape, s: jax.random.normal(k, shape, f32) * s
    gain = lambda k, shape: 1.0 + 0.02 * jax.random.normal(k, shape, f32)
    L = DEPTH
    return {
        "x": nrm(ks[0], (BATCH, SEQ, D_MODEL), 1.0),
        "c": nrm(ks[1], (BATCH, D_MODEL), 1.0),
        "ctx": nrm(ks[2], (BATCH, CTX_LEN, D_MODEL), 1.0),
        "c_ctx": nrm(ks[3], (D_MODEL,), 1.0),
        "w_mod": nrm(ks[4], (L, D_MODEL, 6 * D_MODEL), 0.5 * D_MODEL ** -0.5),
        "b_mod": nrm(ks[5], (L, 6 * D_MODEL), 0.02),
        "g_norm1": gain(ks[6], (L, D_MODEL)),
        "w_in": nrm(ks[7], (L, D_MODEL, D_IN), D_MODEL ** -0.5),
        "w_gate": nrm(ks[8], (L, D_MODEL, N_BRANCH * D_MODEL), D_MODEL ** -0.5),
        "b_gate": nrm(ks[9], (L, N_BRANCH * D_MODEL), 0.02),
        "g_q_gqa": gain(ks[10], (L, HEAD_DIM)),
        "g_k_gqa": gain(ks[11], (L, HEAD_DIM)),
        "g_q_diff": gain(ks[12], (L, HEAD_DIM)),
        "g_k_diff": gain(ks[13], (L, HEAD_DIM)),
        "lambda_q1": nrm(ks[14], (L, HEAD_DIM), 0.1),
        "lambda_k1": nrm(ks[15], (L, HEAD_DIM), 0.1),
        "lambda_q2": nrm(ks[16], (L, HEAD_DIM), 0.1),
        "lambda_k2": nrm(ks[17], (L, HEAD_DIM), 0.1),
        "g_subln": gain(ks[18], (L, DIFF_V_DIM)),
        "w_dw": nrm(ks[19], (L, CONV_WIDTH, CONV_CH), CONV_WIDTH ** -0.5),
        "b_dw": nrm(ks[20], (L, CONV_CH), 0.02),
        "g_conv_ln": gain(ks[21], (L, CONV_CH)),
        "b_conv_ln": nrm(ks[22], (L, CONV_CH), 0.02),
        "w_a": nrm(ks[23], (L, GQA_Q_W, D_MODEL), GQA_Q_W ** -0.5),
        "w_b": nrm(ks[24], (L, DIFF_V_W, D_MODEL), DIFF_V_W ** -0.5),
        "w_c": nrm(ks[25], (L, CONV_CH, D_MODEL), CONV_CH ** -0.5),
        "w_out": nrm(ks[26], (L, D_MODEL, D_MODEL), D_MODEL ** -0.5),
        "g_norm2": gain(ks[27], (L, D_MODEL)),
        "w_ffn_in": nrm(ks[28], (L, D_MODEL, 2 * D_FF), D_MODEL ** -0.5),
        "w_ffn_out": nrm(ks[29], (L, D_FF, D_MODEL), D_FF ** -0.5),
    }

def reference(x, c, ctx, c_ctx, w_mod, b_mod, g_norm1, w_in, w_gate, b_gate,
              g_q_gqa, g_k_gqa, g_q_diff, g_k_diff,
              lambda_q1, lambda_k1, lambda_q2, lambda_k2, g_subln,
              w_dw, b_dw, g_conv_ln, b_conv_ln, w_a, w_b, w_c, w_out,
              g_norm2, w_ffn_in, w_ffn_out):
    n_lat = x.shape[1]
    rope = axial_rope_tables(n_lat)
    xc = ctx
    for l in range(DEPTH):
        last = l == DEPTH - 1
        lam_init = 0.8 - 0.6 * math.exp(-0.3 * l)
        lam = (jnp.exp(jnp.sum(lambda_q1[l].astype(jnp.float32) * lambda_k1[l].astype(jnp.float32)))
               - jnp.exp(jnp.sum(lambda_q2[l].astype(jnp.float32) * lambda_k2[l].astype(jnp.float32)))
               + lam_init)
        mod = jax.nn.silu(c) @ w_mod[l] + b_mod[l]
        sh1, sc1, gt1, sh2, sc2, gt2 = jnp.split(mod[:, None, :], 6, axis=-1)
        mod_c = jax.nn.silu(c_ctx) @ w_mod[l] + b_mod[l]
        csh1, csc1, cgt1, csh2, csc2, cgt2 = jnp.split(mod_c, 6, axis=-1)
        qk_gains = (g_q_gqa[l], g_k_gqa[l], g_q_diff[l], g_k_diff[l])
        branch_w = (g_subln[l], w_a[l], w_b[l], w_dw[l], b_dw[l], g_conv_ln[l], b_conv_ln[l], w_c[l],
                    w_gate[l], b_gate[l], w_out[l])

        h = modulate(rms_norm(x, g_norm1[l]), sh1, sc1)
        hc = modulate(rms_norm(xc, g_norm1[l]), csh1, csc1)
        gq, gk, gv, dq, dk, dv, cu = project_heads(h @ w_in[l], *qk_gains, rope)
        gqc, gkc, gvc, dqc, dkc, dvc, cuc = project_heads(hc @ w_in[l], *qk_gains, None)
        gk_all = jnp.concatenate([gkc, gk], axis=1)
        gv_all = jnp.concatenate([gvc, gv], axis=1)
        dk_all = jnp.concatenate([dkc, dk], axis=1)
        dv_all = jnp.concatenate([dvc, dv], axis=1)
        o_gqa = blocked_queries(lambda qb: gqa_attend(qb, gk_all, gv_all), gq)
        o_diff = blocked_queries(lambda qb: diff_attend(qb, dk_all, dv_all, lam), dq)
        y = merge_branches(h, o_gqa, o_diff, cu, lam_init, *branch_w)
        if not last:
            oc_gqa = gqa_attend(gqc, gkc, gvc)
            oc_diff = diff_attend(dqc, dkc, dvc, lam)
            yc = merge_branches(hc, oc_gqa, oc_diff, cuc, lam_init, *branch_w)
        x = x + gt1 * y
        if not last:
            xc = xc + cgt1 * yc

        x = x + gt2 * swiglu(modulate(rms_norm(x, g_norm2[l]), sh2, sc2), w_ffn_in[l], w_ffn_out[l])
        if not last:
            xc = xc + cgt2 * swiglu(modulate(rms_norm(xc, g_norm2[l]), csh2, csc2),
                                    w_ffn_in[l], w_ffn_out[l])
    return x


_drawn_inputs = setup_inputs


def setup_inputs(seed=0):
    import zlib

    import numpy as np

    out = dict(_drawn_inputs(seed))
    spreads = {}
    factors = {'g_norm1': 8.0,
     'b_gate': 8.0,
     'g_q_gqa': 8.0,
     'g_k_gqa': 8.0,
     'g_q_diff': 8.0,
     'g_k_diff': 8.0,
     'lambda_q1': 3.426,
     'lambda_k1': 4.061,
     'lambda_q2': 3.51,
     'lambda_k2': 4.711,
     'g_subln': 8.0,
     'b_dw': 8.0,
     'g_conv_ln': 8.0,
     'b_conv_ln': 8.0,
     'g_norm2': 6.657}
    for name, (base, spread) in spreads.items():
        noise = np.random.default_rng([zlib.crc32(name.encode()), seed]).standard_normal(out[name].shape)
        drawn = base * np.exp(spread * noise) if base else spread * noise
        out[name] = __import__('jax').numpy.asarray(drawn.astype(out[name].dtype))
    for name, factor in factors.items():
        out[name] = (out[name] * factor).astype(out[name].dtype)
    return out
```

```python
from contextlib import ExitStack, contextmanager
import math

import numpy as np
import concourse.bass as bass
from concourse import mybir

F32 = mybir.dt.float32
F32R = mybir.dt.float32r
ALU = mybir.AluOpType
ACT = mybir.ActivationFunctionType
AX_X = mybir.AxisListType.X

P = 128
D = 1024
KC = D // P
DEPTH = 2
LAT, CTX = 512, 256
TOK = LAT + CTX
HEAD = 64
GRID_W = 64
THETA = 10000.0
EPS = 1e-6
CONV_CH, TAPS = 512, 31
CC = CONV_CH // P
PAD = TAPS // 2
TAPS4 = 8
UW = PAD + LAT + PAD + CTX + PAD + 1
D_FF = 2816
FC = D_FF // P
IN_TILES = 26
GROUPS = [(0, 8), (8, 8), (16, 6)]
MOD_TILES = 48
MOD_RING = 6
SH1, SC1, GT1, SH2, SC2, GT2 = range(6)

V_C = 0
V_BMOD = V_C + KC * 2
V_G = V_BMOD + DEPTH * MOD_TILES * 2
V_BGATE = V_G + DEPTH * 2 * KC * 2
V_GQK = V_BGATE + DEPTH * 24
V_GSUB = V_GQK + DEPTH * 4
V_BDW = V_GSUB + DEPTH
V_GLN = V_BDW + DEPTH * CC
V_BLN = V_GLN + DEPTH * CC
V_LAM = V_BLN + DEPTH * CC
VECS = V_LAM + DEPTH * 4 * HEAD
K_COS, K_SIN, K_ONES, K_BLOCK, K_ID = 0, LAT, 2 * LAT, 2 * LAT + P, 2 * LAT + 2 * P
CONSTS = 2 * LAT + 3 * P


class Counts:

    def __init__(self):
        self.n, self.loops = {}, []

    def at(self, name, off=0):
        v = self.n.get(name, 0) + off
        for i, per in self.loops:
            if per.get(name):
                v = i * per[name] + v
        return v

    def pair(self, name, off=0):
        k = self.n.get(name, 0) + off
        v = k // 2
        for i, per in self.loops:
            assert per.get(name, 0) % 2 == 0, name
            if per.get(name):
                v = i * (per[name] // 2) + v
        return k % 2, v

    def step(self, name, k=1):
        self.n[name] = self.n.get(name, 0) + k

    @contextmanager
    def repeat(self, eng, n, per):
        before = dict(self.n)
        with eng.Fori(0, n) as i:
            self.loops.append((i, per))
            yield i
            self.loops.pop()
        for name in set(self.n) | set(per):
            moved = self.n.get(name, 0) - before.get(name, 0)
            assert moved in (0, per.get(name, 0)), (name, moved, per.get(name, 0))
            self.n[name] = before.get(name, 0) + n * per.get(name, 0)


def stream_pieces(a, n):
    if a < LAT < a + n:
        return [(a, LAT - a, 0), (LAT, a + n - LAT, 1)]
    return [(a, n, 0 if a < LAT else 1)]


def build(nc, xT, vecs, consts, wdw, w_mod, w_in, w_gate, w_br, w_out, w_fi, w_fo, out):
    x_next = nc.dram_tensor("x_next", (P, KC, LAT), F32).ap()

    with ExitStack() as ctx:
        def sb(name, shape, dt):
            return ctx.enter_context(nc.sbuf_tensor(name, shape, dt))

        sems = {}

        def S(name):
            if name not in sems:
                sems[name] = ctx.enter_context(nc.semaphore("s_" + name))
            return sems[name]

        H = sb("H", [P, 2, KC, TOK], F32R)
        RB = sb("RB", [P, 2 * KC * TOK], F32R)
        WHI = sb("WHI", [P, 2, KC * P], F32R)
        WLO = sb("WLO", [P, 2, KC * P], F32R)
        STG = sb("STG", [P, 2, KC * P], F32)
        X = sb("X", [P, KC, TOK], F32)
        M = sb("M", [P, KC * TOK + 768], F32)
        U = sb("U", [P, CC * UW], F32)
        G = sb("G", [P, TOK], F32)
        T = sb("T", [P, TOK], F32)
        R = sb("R", [P, TOK], F32)
        V = sb("V", [P, VECS], F32)
        K = sb("K", [P, CONSTS], F32)
        WDW = sb("WDW", [P, DEPTH, CC, 4 * TAPS4], F32)
        MOD = sb("MOD", [P, DEPTH, 6, KC, 2], F32)
        A = sb("A", [P, DEPTH, 2, KC, 2], F32)
        SC = sb("SC", [P, KC, 2], F32)
        LM = sb("LM", [P, 16], F32)
        NEGLAM = sb("NEGLAM", [P, DEPTH], F32)
        GS = sb("GS", [P, DEPTH], F32)
        EC = sb("EC", [P, 4], F32)
        NM = sb("NM", [P, 4], F32)
        L = sb("L", [P, 4], F32)
        RL = sb("RL", [P, 4], F32)
        RLN = sb("RLN", [P, 2], F32)

        v4 = lambda t, o, a, b: t[:, o:o + a * b].rearrange("p (a b) -> p a b", b=b)
        cat = lambda t, k, n=TOK: v4(t, k * n, 1, n)[:, 0, :]
        QK = RB[:, 0:4 * TOK].rearrange("p (w s t) -> p w s t", w=2, s=2)
        VT = RB[:, 4 * TOK:6 * TOK].rearrange("p (s k d) -> p s k d", s=2, k=6)
        PT = RB[:, 6 * TOK:6 * TOK + 4 * 1536].rearrange("p (b s k q) -> p b s k q", b=2, s=2, k=6)
        BR = RB[:, :].rearrange("p (s k t) -> p s k t", s=2, k=KC)
        MM = M[:, 0:KC * TOK].rearrange("p (k t) -> p k t", k=KC)
        PR = M[:, 0:4 * TOK].rearrange("p (n t) -> p n t", n=4)
        XG = M[:, 4 * TOK:6 * TOK].rearrange("p (n t) -> p n t", n=2)
        XS = M[:, 6 * TOK:8 * TOK].rearrange("p (n t) -> p n t", n=2)
        OSQ = M[:, 8 * TOK:9 * TOK].rearrange("p (n q) -> p n q", n=3)
        MODR = M[:, 0:MOD_RING * KC * P].rearrange("p (n w) -> p n w", n=MOD_RING)
        COS, SIN = K[:, K_COS:K_COS + LAT], K[:, K_SIN:K_SIN + LAT]
        ONES, BLOCK, IDENT = (K[:, o:o + P] for o in (K_ONES, K_BLOCK, K_ID))

        ps = lambda n, w: ctx.enter_context(nc.psum_tensor(n, [P, w], F32))
        acc = [ps("acc0", 512), ps("acc1", 512)]
        aux = [ps("aux0", 512), ps("aux1", 512)]
        sco = [ps("sco0", 1024), ps("sco1", 1024)]

        def n_tok(l):
            return TOK if l == 0 else LAT

        def ranges(l, wide):
            if l == 0:
                return [(0, 384), (384, 384)]
            return [(0, LAT), (LAT, CTX)] if wide else [(0, LAT)]

        def blocks(l):
            return [(0, 0), (256, 0)] + ([(LAT, 4)] if l == 0 else [])

        def qtiles(l):
            return [(q, k0, n) for n, (c0, k0) in enumerate(blocks(l)) for q in (c0, c0 + 128)]

        def halves(n):
            return [(0, n // 2), (n // 2, n // 2)]

        nr = lambda l: len(ranges(l, False))
        nb = lambda l: len(blocks(l))
        aux_att = lambda l: sum(2 if k0 == 0 else 1 for _, k0, _ in qtiles(l))

        def per_gqa(l):
            return dict(tile=2, acc=2 * nr(l) + 2 * nb(l), aux=2 + 2 * aux_att(l),
                        xs=nr(l), ln=2, rs=1, y=1, qk=1, rope=3, xg0=1, xg1=0,
                        sc=4 * nb(l), pn=4 * nb(l), rl=0, pb=0, pth=2 * aux_att(l), pt=2 * aux_att(l),
                        recip=4 * nb(l), qhi=1)

        def per_diff(l):
            return dict(tile=4, acc=2 * nr(l) + 4 + 2 * nb(l), aux=2 + 2 + 2 + aux_att(l),
                        xs=nr(l) + 2, ln=4, rs=2, y=2, qk=2, rope=6, xg0=2, xg1=2,
                        sc=4 * nb(l), pn=2 * nb(l), rl=4 * nb(l) // 2, pb=2 * nb(l),
                        pth=aux_att(l), pt=aux_att(l), recip=2 * nb(l), qhi=2,
                        vev=2, vhi=2, vlo=2, sg=nr(l), glu=sum(len(stream_pieces(a, w)) for a, w in ranges(l, False)), osq=nb(l), orl=nb(l), orr=nb(l), od=nb(l))

        def per_merge(l):
            return dict(tile=2, acc=2 * nr(l), g=nr(l))

        def per_out(l):
            return dict(tile=2, acc=2 * nr(l))

        def per_ffn(l):
            return dict(tile=2, acc=2 * nr(l), g=nr(l), mt=nr(l), midh=nr(l), mid_chunks=1, mid_half=nr(l) - 1)

        def conv_width(l):
            return UW - TAPS if l == 0 else LAT

        def conv_halves(l):
            w = conv_width(l)
            return [(0, w // 2 + w % 2), (w // 2 + w % 2, w // 2)]

        def conv_pieces(a, n):
            return [(s, s if t == 0 else s + PAD, w) for s, w, t in stream_pieces(a, n)]

        XW = UW - TAPS
        X1 = X[:, :, :].rearrange("p k t -> p (k t)")

        def XC(l, ch):
            return X1[:, ch * XW:ch * XW + conv_width(l)]

        def US(l, ch):
            return U[:, ch * UW:ch * UW + conv_width(l)]

        block = ctx.enter_context(nc.Block())

        @block.sync
        def _(sp):
            c = Counts()

            def tile(src, n):
                s, _ = c.pair("tile")
                dst = STG[:, s, 0:n]
                sp.wait_ge(S("w_split"), c.at("tile") + 1)
                sp.dma_start(dst, src).then_inc(S(f"w_load{s}"), 16)
                c.step("tile")

            sp.dma_start(V[:, :], vecs).then_inc(S("vecs"), 16)
            sp.dma_start(K[:, :], consts).then_inc(S("consts"), 16)
            sp.dma_start(WDW[:, :, :, 0:TAPS], wdw).then_inc(S("wdw"), 16)
            sp.dma_start(X[:, :, :], xT).then_inc(S("x"), 16)
            with c.repeat(sp, DEPTH * MOD_TILES // MOD_RING, dict(mod=MOD_RING)) as i:
                for s in range(MOD_RING):
                    src = w_mod[i * MOD_RING + s]
                    sp.wait_ge(S("mod_used"), c.at("mod") + 1)
                    sp.dma_start(MODR[:, s, :], src).then_inc(S(f"mod_load{s}"), 16)
                    c.step("mod")
            for l in range(DEPTH):
                tile(w_in[l, 0], KC * P)
                tile(w_in[l, 1], KC * P)
                with c.repeat(sp, 4, per_gqa(l)) as j:
                    for s in range(2):
                        tile(w_in[l, j * 2 + (2 + s)], KC * P)
                with c.repeat(sp, 4, per_diff(l)) as h:
                    for s in range(4):
                        tile(w_in[l, h * 4 + (10 + s)], KC * P)
                for b in range(3):
                    with c.repeat(sp, KC, per_merge(l)) as j:
                        tile(w_gate[l, j + b * KC], KC * P)
                        tile(w_br[l, j + b * KC], CC * P)
                    if b == 2:
                        sp.wait_ge(S("c_split"), CC * (l + 1))
                        if l == 0:
                            sp.dma_start(X[:, :, :], xT).then_inc(S("x"), 16)
                        else:
                            sp.dma_start(X[:, :, 0:LAT], x_next).then_inc(S("x"), 16)
                with c.repeat(sp, 4, per_out(l)) as j:
                    for s in range(2):
                        tile(w_out[l, j * 2 + s], KC * P)
                for k0, n in GROUPS:
                    with c.repeat(sp, n, per_ffn(l)) as f:
                        for s in range(2):
                            tile(w_fi[l, f * 2 + (2 * k0 + s)], KC * P)
                    with c.repeat(sp, 4, per_out(l)) as j:
                        for s in range(2):
                            tile(w_fo[l, j * 2 + s][:, k0 * P:(k0 + n) * P], n * P)
                sp.wait_ge(S("x_done"), l + 1)
                if l == 0:
                    sp.dma_start(x_next, X[:, :, 0:LAT]).then_inc(S("saved"), 16)
                    sp.wait_ge(S("saved"), 16)
                    sp.sem_inc(S("x_saved"), 1)
                else:
                    sp.dma_start(out, X[:, :, 0:LAT]).then_inc(S("stored"), 16)
                    sp.wait_ge(S("stored"), 16)

        @block.gpsimd
        def _(pool):
            c = Counts()

            def split(n):
                s, _ = c.pair("tile")
                pool.wait_ge(S("w_hi"), c.at("tile") + 1)
                nc.gpsimd.tensor_tensor(WLO[:, s, 0:n], STG[:, s, 0:n], WHI[:, s, 0:n].bitcast(F32),
                                        ALU.subtract).then_inc(S("w_split"), 1)
                c.step("tile")

            pool.sem_inc(S("w_split"), 2)
            nc.gpsimd.memset(U[:, :], 0.0).then_inc(S("u_zero"), 1)
            nc.gpsimd.memset(EC[:, 0:1], EPS).then_inc(S("ec"), 1)
            nc.gpsimd.memset(EC[:, 1:2], HEAD * EPS).then_inc(S("ec"), 1)
            nc.gpsimd.memset(EC[:, 2:3], 0.0).then_inc(S("ec"), 1)
            nc.gpsimd.memset(WDW[:, :, :, TAPS:4 * TAPS4], 0.0).then_inc(S("wdw_zero"), 1)
            for l in range(DEPTH):
                split(KC * P)
                split(KC * P)
                with c.repeat(pool, 4, per_gqa(l)):
                    for s in range(2):
                        split(KC * P)
                with c.repeat(pool, 4, per_diff(l)):
                    for s in range(4):
                        split(KC * P)
                for b in range(3):
                    with c.repeat(pool, KC, per_merge(l)):
                        split(KC * P)
                        split(CC * P)
                with c.repeat(pool, 4, per_out(l)):
                    for s in range(2):
                        split(KC * P)
                for k0, n in GROUPS:
                    with c.repeat(pool, n, per_ffn(l)):
                        for s in range(2):
                            split(KC * P)
                    with c.repeat(pool, 4, per_out(l)):
                        for s in range(2):
                            split(n * P)

        @block.tensor
        def _(pe):
            c = Counts()

            def open_acc():
                b, n = c.pair("acc")
                pe.wait_ge(S(f"acc_free{b}"), n + 1)
                return acc[b]

            def close_acc(mm):
                mm.then_inc(S("acc_full"), 1)
                c.step("acc")

            def open_aux():
                b, n = c.pair("aux")
                pe.wait_ge(S(f"aux_free{b}"), n + 1)
                return aux[b]

            def close_aux(mm):
                mm.then_inc(S("aux_full"), 1)
                c.step("aux")

            def product(dst, lh, ll, rh, rl, first, last):
                nc.tensor.matmul(dst, lh, rh, start=first, stop=False)
                nc.tensor.matmul(dst, lh, rl, start=False, stop=False)
                return nc.tensor.matmul(dst, ll, rh, start=False, stop=last)

            def tile(kn, moving, rngs, ready=None, between=None):
                s, _ = c.pair("tile")
                pe.wait_ge(S("w_split"), c.at("tile") + 3)
                for n, (a, w) in enumerate(rngs):
                    dst = open_acc()
                    for k in range(kn):
                        if ready and n == 0:
                            pe.wait_ge(S(ready[0]), ready[1] + k + 1)
                        if between and n == len(rngs) - 1 and k == kn // 2:
                            between()
                        mm = product(dst[:, 0:w], WHI[:, s, k * P:(k + 1) * P], WLO[:, s, k * P:(k + 1) * P],
                                     moving[:, 0, k, a:a + w], moving[:, 1, k, a:a + w], k == 0, k == kn - 1)
                    close_acc(mm)
                pe.wait_ge(S("acc_full"), c.at("acc"))
                pe.sem_inc(S("w_used"), 1)
                c.step("tile")

            def head_sums(p, n, seen):
                c.step("xs", seen)
                pe.wait_ge(S("xs"), c.at("xs"))
                for a, w in halves(n):
                    close_aux(nc.tensor.matmul(open_aux()[:, 0:w], BLOCK, XS[:, p, a:a + w], start=True, stop=True))

            def turn_v(p):
                c.step("vev", 2)
                pe.wait_ge(S("vev"), c.at("vev"))
                for a in range(2):
                    dst = open_aux()
                    for k in range(3):
                        t = nc.tensor.transpose(dst[:, k * P:(k + 1) * P], XG[:, p, (3 * a + k) * P:(3 * a + k + 1) * P], IDENT)
                    close_aux(t)

            def score(side, q, k0):
                s, n = c.pair("sc")
                pe.wait_ge(S("exp"), c.at("sc") + 1)
                h = slice(side * HEAD, side * HEAD + HEAD)
                for a, w, o in ([(0, LAT, 0), (LAT, CTX, LAT)] if k0 == 0 else [(LAT, CTX, 0)]):
                    mm = product(sco[s][:, o:o + w], QK[h, 0, 0, q:q + P], QK[h, 0, 1, q:q + P],
                                 QK[h, 1, 0, a:a + w], QK[h, 1, 1, a:a + w], True, True)
                mm.then_inc(S("scored"), 1)
                c.step("sc")

            def turn_probs(slot, k0):
                c.step("pn")
                pe.wait_ge(S("pn"), c.at("pn"))
                ks = list(range(k0, 6))
                for part in ([ks[0:3], ks[3:6]] if k0 == 0 else [ks]):
                    dst = open_aux()
                    for n, k in enumerate(part):
                        t = nc.tensor.transpose(dst[:, n * P:(n + 1) * P], PR[:, slot, (k - k0) * P:(k - k0 + 1) * P], IDENT)
                    close_aux(t)

            def weigh(blk, k0, due):
                c.step("pt", due)
                pe.wait_ge(S("pt"), c.at("pt"))
                dst = open_acc()
                for k in range(k0, 6):
                    mm = product(dst[:, 0:256], VT[:, 0, k, :], VT[:, 1, k, :],
                                 PT[:, blk % 2, 0, k, :], PT[:, blk % 2, 1, k, :], k == k0, k == 5)
                close_acc(mm)

            def sub_sums(blk):
                c.step("osq")
                pe.wait_ge(S("osq"), c.at("osq"))
                close_acc(nc.tensor.matmul(open_acc()[:, 0:256], ONES, OSQ[:, blk % 3, :], start=True, stop=True))

            def norm_sums(n, wait):
                wait()
                for a, w in halves(n):
                    close_acc(nc.tensor.matmul(open_acc()[:, 0:w], ONES, MM[:, 0, a:a + w], start=True, stop=True))

            def norm(l, k, n):
                c.step("nadd", KC - 1)
                norm_sums(n, lambda: pe.wait_ge(S("nadd"), c.at("nadd")))

            def attention_items(l, maps):
                if maps == 1:
                    return [(hp, q, k0, hp * nb(l) + n) for hp in range(2) for q, k0, n in qtiles(l)]
                return [(0, q, k0, n) for q, k0, n in qtiles(l)]

            pe.sem_inc(S("w_used"), 2)
            pe.sem_inc(S("mod_used"), MOD_RING)
            pe.wait_ge(S("silu_c"), 1)
            with c.repeat(pe, DEPTH * MOD_TILES // MOD_RING, dict(mod=MOD_RING, modl=16)) as i:
                for s in range(MOD_RING):
                    pe.wait_ge(S(f"mod_load{s}"), c.at("modl", 16))
                    for k in range(KC):
                        mm = nc.tensor.matmul(sco[0][:, bass.ds((i * MOD_RING + s) * 2, 2)], MODR[:, s, k * P:(k + 1) * P],
                                              SC[:, k, :], start=(k == 0), stop=(k == KC - 1))
                    mm.then_inc(S("mod_used"), 1)
            for l in range(DEPTH):
                norm(l, 0, TOK)
                wide, slim = ranges(l, True), ranges(l, False)
                n = n_tok(l)
                tile(KC, H, wide, ready=("h_ready", 2 * KC * l))
                tile(KC, H, wide, between=lambda: head_sums(1, TOK, 2))
                turn_v(0)
                c.step("vlo", 2)
                pe.wait_ge(S("vlo"), c.at("vlo"))
                for maps, per in ((1, per_gqa(l)), (2, per_diff(l))):
                    if maps == 1:
                        c.step("qk", 1)
                    with c.repeat(pe, 4, per):
                        if maps == 1:
                            tile(KC, H, slim)
                            tile(KC, H, slim, between=lambda: head_sums(0, n, nr(l)))
                            c.step("qk", 1)
                        else:
                            tile(KC, H, slim)
                            tile(KC, H, wide, between=lambda: head_sums(0, n, nr(l)))
                            tile(KC, H, wide, between=lambda: head_sums(1, TOK, 2))
                            tile(KC, H, slim, between=lambda: turn_v(0))
                            c.step("qk", 2)
                            c.step("vlo", 2)
                            pe.wait_ge(S("vlo"), c.at("vlo"))
                        pe.wait_ge(S("qk"), c.at("qk"))
                        items = attention_items(l, maps)
                        ahead = 2 if maps == 1 else 1

                        def scores(i):
                            side, q, k0, _ = items[i]
                            for m in range(maps):
                                score(side if maps == 1 else m, q, k0)

                        done = 0
                        for i in range(ahead):
                            scores(i)
                        for i, (side, q, k0, blk) in enumerate(items):
                            if i + ahead < len(items):
                                scores(i + ahead)
                            turn_probs((i * maps) % 4, k0)
                            if (i % 2 == 0 and i) or i == len(items) - 1:
                                for blk in ([i // 2 - 1] if i % 2 == 0 else [i // 2]):
                                    k0 = items[2 * blk][2]
                                    if maps == 2 and blk:
                                        sub_sums(blk - 1)
                                    weigh(blk, k0, 4 if k0 == 0 else 2)
                        if maps == 2:
                            sub_sums(nb(l) - 1)
                for b in range(3):
                    for j in range(1):
                        with c.repeat(pe, KC, per_merge(l)):
                            tile(KC, H, slim)
                            tile(CC, BR[:, :, 4 * (b % 2):4 * (b % 2) + 4, :], slim,
                                 ready=(("bsplit", 8 * l + 4 * b) if b < 2 else ("c_split", CC * l)))
                    if b == 1:
                        w = LAT if l == 0 else LAT // 2
                        for k in range(2):
                            c.step("lsum")
                            pe.wait_ge(S("lsum"), c.at("lsum"))
                            for a, w in conv_halves(l):
                                close_acc(nc.tensor.matmul(open_acc()[:, 0:w], ONES, U[:, a:a + w], start=True, stop=True))
                with c.repeat(pe, 4, per_out(l)):
                    for s in range(2):
                        tile(KC, H, slim, ready=("msplit", KC * l))
                norm(l, 1, n)
                for g, (k0, m) in enumerate(GROUPS):
                    with c.repeat(pe, m, per_ffn(l)):
                        for s in range(2):
                            tile(KC, H, slim, ready=(("h_ready", 2 * KC * l + KC) if s == 0 and g == 0 else None))
                    with c.repeat(pe, 4, per_out(l)):
                        for s in range(2):
                            tile(m, BR, slim, ready=("mid_chunks", 1 + FC * l + k0) if s == 0 else None)

        @block.scalar
        def _(act):
            c = Counts()

            def wait_acc():
                b, n = c.pair("acc")
                act.wait_ge(S("acc_full"), c.at("acc") + 1)
                c.step("acc")
                return b

            def wait_aux():
                b, n = c.pair("aux")
                act.wait_ge(S("aux_full"), c.at("aux") + 1)
                c.step("aux")
                return b

            def settle():
                act.sem_inc(S("act_turn"), 1)

            def hi(n=KC * P):
                s, k = c.pair("tile")
                act.wait_ge(S(f"w_load{s}"), k * 16 + 16)
                act.wait_ge(S("w_used"), c.at("tile") + 1)
                nc.scalar.activation(WHI[:, s, 0:n], STG[:, s, 0:n], ACT.Copy).then_inc(S("w_hi"), 1)
                c.step("tile")

            def fn(dst, src, f, sem=None, **kw):
                ins = nc.scalar.activation(dst, src, f, **kw)
                if sem:
                    ins.then_inc(S(sem), 1)
                return ins

            def exp_set():
                nc.scalar.preload_act_table_set("natural_log_exp_and_others")

            def evac_norm(l, p, rngs, g):
                act.wait_ge(S(f"xg_free{p}"), c.at(f"xg{p}") + 1)
                for a, w in rngs:
                    b = wait_acc()
                    fn(XG[:, p, a:a + w], acc[b][:, 0:w], ACT.Identity, scale=V[:, V_GQK + 4 * l + g:V_GQK + 4 * l + g + 1], bias=EC[:, 2:3], sem="xgw")
                    fn(XS[:, p, a:a + w], acc[b][:, 0:w], ACT.Square, sem=f"acc_free{b}")
                    act.wait_ge(S(f"acc_free{b}"), c.pair("acc", -1)[1] + 2)
                    act.sem_inc(S("xs"), 1)
                c.step(f"xg{p}")

            def finish_norm(p, n, is_q):
                act.wait_ge(S("rs_free"), c.at("rs") + 1)
                for a, w in halves(n):
                    b = wait_aux()
                    fn(R[:, a:a + w], aux[b][:, 0:w], ACT.Ln, scale=1.0 if is_q else 1.0 / HEAD,
                       bias=EC[:, 1:2] if is_q else EC[:, 0:1], sem=f"aux_free{b}")
                    act.wait_ge(S(f"aux_free{b}"), c.pair("aux", -1)[1] + 2)
                fn(R[:, 0:n], R[:, 0:n], ACT.Exp, scale=-0.5, sem="rs")
                c.step("rs")
                c.step("y")
                act.wait_ge(S("y"), c.at("y"))
                fn(QK[:, 0 if is_q else 1, 0, 0:n], XG[:, p, 0:n], ACT.Copy, sem="qhi")

            def evac_v(p, rngs):
                act.wait_ge(S(f"xg_free{p}"), c.at(f"xg{p}") + 1)
                for a, w in rngs:
                    b = wait_acc()
                    fn(XG[:, p, a:a + w], acc[b][:, 0:w], ACT.Copy, sem=f"acc_free{b}")
                    act.wait_ge(S(f"acc_free{b}"), c.pair("acc", -1)[1] + 2)
                    act.sem_inc(S("vev"), 1)
                c.step(f"xg{p}")

            def finish_v():
                for a in range(2):
                    b = wait_aux()
                    fn(VT[:, 0, 3 * a:3 * a + 3, :], v4(aux[b], 0, 3, P), ACT.Copy, sem="vhi")

            def evac_conv_a(l, ch, rngs):
                act.wait_ge(S("u_zero"), l + 1)
                for a, w in rngs:
                    b = wait_acc()
                    ps_ = conv_pieces(a, w)
                    for k, (s, o, m) in enumerate(ps_):
                        settle()
                        fn(U[:, bass.ds(ch * UW + (PAD + o), m)], acc[b][:, s - a:s - a + m], ACT.Copy,
                           sem=f"acc_free{b}" if k == len(ps_) - 1 else "ua")

            def evac_conv_g(p, rngs):
                act.wait_ge(S(f"xg_free{p}"), c.at(f"xg{p}") + 1)
                for a, w in rngs:
                    b = wait_acc()
                    fn(XS[:, p, a:a + w], acc[b][:, 0:w], ACT.Sigmoid, sem=f"acc_free{b}")
                    act.wait_ge(S(f"acc_free{b}"), c.pair("acc", -1)[1] + 2)
                    act.sem_inc(S("sg"), 1)
                c.step(f"xg{p}")

            def exp(k, k0):
                s, _ = c.pair("sc")
                slot = k % 4
                n = TOK if k0 == 0 else CTX
                act.wait_ge(S("max"), c.at("sc") + 1)
                fn(PR[:, slot, 0:n], sco[s][:, 0:n], ACT.Exp, bias=NM[:, slot:slot + 1], accum_out=L[:, slot:slot + 1], sem="exp")
                c.step("sc")

            def turned_hi(blk, half, k0):
                for a in range(2 if k0 == 0 else 1):
                    b = wait_aux()
                    kk = slice(3 * a, 3 * a + 3) if k0 == 0 else slice(4, 6)
                    m = 3 if k0 == 0 else 2
                    fn(PT[:, blk % 2, 0, kk, half * P:half * P + P], v4(aux[b], 0, m, P), ACT.Copy, sem="pth")

            def norm(l, k, n):
                exp_set()
                for j in range(KC):
                    fn(MM[:, j, 0:n], X[:, j, 0:n], ACT.Square, sem="nsq")
                for i, (a, w) in enumerate(halves(n)):
                    b = wait_acc()
                    fn(R[:, a:a + w], acc[b][:, 0:w], ACT.Ln, scale=1.0 / D, bias=EC[:, 0:1], sem=f"acc_free{b}")
                    act.wait_ge(S(f"acc_free{b}"), c.pair("acc", -1)[1] + 2)
                fn(R[:, 0:n], R[:, 0:n], ACT.Exp, scale=-0.5, sem="nrs")
                for j in range(KC):
                    c.step("ntm")
                    act.wait_ge(S("ntm"), c.at("ntm"))
                    for a, w, s in stream_pieces(0, n):
                        sh = MOD[:, l, SH1 if k == 0 else SH2, j, s:s + 1]
                        fn(MM[:, j, a:a + w], MM[:, j, a:a + w], ACT.Identity, scale=A[:, l, k, j, s:s + 1], bias=sh, sem="naf")
                        c.step("naf")
                    act.wait_ge(S("naf"), c.at("naf"))
                    fn(H[:, 0, j, 0:n], MM[:, j, 0:n], ACT.Copy, sem="nhi")

            act.sem_inc(S("exp"), 2)
            act.sem_inc(S("acc_free0"), 1)
            act.sem_inc(S("acc_free1"), 1)
            act.sem_inc(S("aux_free0"), 1)
            act.sem_inc(S("aux_free1"), 1)
            act.wait_ge(S("vecs"), 16)
            act.wait_ge(S("ec"), 3)
            fn(SC[:, :, :], v4(V, V_C, KC, 2), ACT.Silu, sem="silu_c")
            exp_set()
            c.step("lam", 2)
            act.wait_ge(S("lam"), 4)
            fn(LM[:, 8:12], LM[:, 0:4], ACT.Exp, sem="lam_exp")
            act.wait_ge(S("x"), 16)
            act.wait_ge(S("mod_ready"), 1)
            hi()
            for l in range(DEPTH):
                wide, slim = ranges(l, True), ranges(l, False)
                n = n_tok(l)
                if l:
                    act.wait_ge(S("x_done"), l)
                norm(l, 0, TOK)
                hi()
                evac_norm(l, 1, wide, 1)
                hi()
                evac_v(0, wide)
                finish_norm(1, TOK, False)
                finish_v()
                if l:
                    act.wait_ge(S("x_saved"), l)
                with c.repeat(act, 4, per_gqa(l)) as j:
                    hi()
                    evac_norm(l, 0, slim, 0)
                    hi()
                    finish_norm(0, n, True)
                    evac_conv_a(l, j, slim)
                    items = [(hp, q, k0, hp * nb(l) + m) for hp in range(2) for q, k0, m in qtiles(l)]
                    exp(0, items[0][2])
                    for i, (hp, q, k0, blk) in enumerate(items):
                        if i + 1 < len(items):
                            exp(i + 1, items[i + 1][2])
                        turned_hi(blk, i % 2, k0)
                        if (i % 2 == 0 and i) or i == len(items) - 1:
                            w = i // 2 - 1 if i % 2 == 0 else i // 2
                            side, q0 = items[2 * w][0], items[2 * w][1]
                            b = wait_acc()
                            rows = slice(side * HEAD, side * HEAD + HEAD)
                            settle()
                            fn(X[rows, j, q0:q0 + 256], acc[b][rows, 0:256], ACT.Copy, sem=f"acc_free{b}")
                with c.repeat(act, 4, per_diff(l)) as h:
                    hi()
                    evac_norm(l, 0, slim, 2)
                    hi()
                    evac_norm(l, 1, wide, 3)
                    finish_norm(0, n, True)
                    hi()
                    evac_v(0, wide)
                    finish_norm(1, TOK, False)
                    hi()
                    finish_v()
                    evac_conv_g(1, slim)
                    exp_set()
                    items = [(0, q, k0, m) for q, k0, m in qtiles(l)]
                    exp(0, items[0][2])
                    exp(1, items[0][2])

                    def sub(w):
                        b = wait_acc()
                        q0 = items[2 * w][1]
                        fn(T[:, q0:q0 + 256], acc[b][:, 0:256], ACT.Ln, scale=1.0 / P, bias=EC[:, 0:1], sem=f"acc_free{b}")
                        act.wait_ge(S(f"acc_free{b}"), c.pair("acc", -1)[1] + 2)
                        fn(T[:, q0:q0 + 256], T[:, q0:q0 + 256], ACT.Exp, scale=-0.5, sem="orr")

                    for i, (_, q, k0, blk) in enumerate(items):
                        slot = (2 * i + 1) % 4
                        nk = TOK if k0 == 0 else CTX
                        c.step("rl")
                        act.wait_ge(S("rl"), c.at("rl"))
                        fn(PR[:, slot, 0:nk], PR[:, slot, 0:nk], ACT.Copy, scale=RLN[:, i % 2:i % 2 + 1], sem="pb")
                        if i + 1 < len(items):
                            exp(2 * i + 2, items[i + 1][2])
                            exp(2 * i + 3, items[i + 1][2])
                        turned_hi(blk, i % 2, k0)
                        if (i % 2 == 0 and i) or i == len(items) - 1:
                            w = i // 2 - 1 if i % 2 == 0 else i // 2
                            if w:
                                sub(w - 1)
                            q0 = items[2 * w][1]
                            b = wait_acc()
                            settle()
                            fn(X[:, h + 4, q0:q0 + 256], acc[b][:, 0:256], ACT.Copy, sem="oraw")
                            fn(OSQ[:, w % 3, :], acc[b][:, 0:256], ACT.Square, sem=f"acc_free{b}")
                            act.wait_ge(S(f"acc_free{b}"), c.pair("acc", -1)[1] + 2)
                            act.sem_inc(S("osq"), 1)
                    sub(nb(l) - 1)
                act.wait_ge(S("od"), 4 * nb(0) * (l > 0) + 4 * nb(l))
                for k in range(KC):
                    fn(BR[:, 0, k, 0:n], X[:, k, 0:n], ACT.Copy, sem="bhi")
                for b in range(3):
                    if b == 0:
                        act.wait_ge(S("bsplit"), 8 * (l + 1))
                        for ch in range(CC):
                            fn(XC(l, ch), U[:, 0:conv_width(l)], ACT.Identity, scale=EC[:, 2:3],
                               bias=V[:, V_BDW + CC * l + ch:V_BDW + CC * l + ch + 1], sem="cbias")
                    with c.repeat(act, KC, per_merge(l)) as j:
                        hi(CC * P)
                        for i, (a, w) in enumerate(slim):
                            bb, m = c.pair("acc", -1 if l else -2)
                            act.wait_ge(S(f"acc_free{bb}"), m + 2)
                            b_ = wait_acc()
                            settle()
                            fn(G[:, a:a + w], acc[b_][:, 0:w], ACT.Sigmoid,
                               bias=V[:, bass.ds(j + (V_BGATE + 24 * l + 8 * b), 1)], sem=f"acc_free{b_}")
                            act.wait_ge(S(f"acc_free{b_}"), c.pair("acc", -1)[1] + 2)
                            act.sem_inc(S("g"), 1)
                        hi()
                        c.step("acc", nr(l))
                    if b == 1:
                        w0 = conv_width(l)
                        exp_set()
                        c.step("acc", 2)
                        for ch in range(CC):
                            c.step("lcen")
                            act.wait_ge(S("lcen"), c.at("lcen"))
                            fn(US(l, ch), XC(l, ch), ACT.Square, sem="lsq")
                        for a, w in conv_halves(l):
                            b_ = wait_acc()
                            fn(U[:, UW + a:UW + a + w], acc[b_][:, 0:w], ACT.Ln, scale=1.0 / CONV_CH, bias=EC[:, 0:1], sem=f"acc_free{b_}")
                            act.wait_ge(S(f"acc_free{b_}"), c.pair("acc", -1)[1] + 2)
                        fn(U[:, UW:UW + w0], U[:, UW:UW + w0], ACT.Exp, scale=-0.5, sem="lrs")
                        for ch in range(CC):
                            o = CC * l + ch
                            c.step("lnx")
                            act.wait_ge(S("lnx"), c.at("lnx"))
                            fn(XC(l, ch), XC(l, ch), ACT.Silu, scale=V[:, V_GLN + o:V_GLN + o + 1], bias=V[:, V_BLN + o:V_BLN + o + 1], sem="lsw")
                            c.step("lsw")
                            act.wait_ge(S("lsw"), c.at("lsw"))
                            for s, o, m in conv_pieces(0, n):
                                fn(BR[:, 0, ch, s:s + m], X1[:, ch * XW + o:ch * XW + o + m], ACT.Copy, sem="chi")
                c.step("mdone", 1)
                act.wait_ge(S("mdone"), c.at("mdone"))
                for k in range(KC):
                    fn(H[:, 0, k, 0:n], MM[:, k, 0:n], ACT.Copy, sem="mhi")
                with c.repeat(act, 4, per_out(l)):
                    for s in range(2):
                        c.step("acc", nr(l))
                        hi()
                c.step("xres", 1)
                act.wait_ge(S("xres"), c.at("xres"))
                norm(l, 1, n)
                for g, (k0, m) in enumerate(GROUPS):
                    with c.repeat(act, m, per_ffn(l)) as f:
                        hi()
                        for i, (a, w) in enumerate(slim):
                            bb, m_ = c.pair("acc", -1 if l else -2)
                            act.wait_ge(S(f"acc_free{bb}"), m_ + 2)
                            b_ = wait_acc()
                            fn(G[:, a:a + w], acc[b_][:, 0:w], ACT.Silu, sem=f"acc_free{b_}")
                            act.wait_ge(S(f"acc_free{b_}"), c.pair("acc", -1)[1] + 2)
                            act.sem_inc(S("g"), 1)
                        hi()
                        for i, (a, w) in enumerate(slim):
                            c.step("acc")
                            c.step("mt")
                            act.wait_ge(S("mt"), c.at("mt"))
                            settle()
                            fn(BR[:, 0, f, a:a + w], T[:, a:a + w], ACT.Copy, sem="midh")
                    last = l == DEPTH - 1 and g == len(GROUPS) - 1
                    with c.repeat(act, 3 if last else 4, per_out(l)):
                        for s in range(2):
                            c.step("acc", nr(l))
                            hi()
                    if last:
                        hi()

        @block.vector
        def _(dve):
            c = Counts()

            def wait_acc():
                b, n = c.pair("acc")
                dve.wait_ge(S("acc_full"), c.at("acc") + 1)
                c.step("acc")
                return b

            def own(name, ins, k=1):
                ins.then_inc(S(name), 1)
                c.step(name)
                dve.wait_ge(S(name), c.at(name))

            def tt(dst, a, b, op):
                return nc.vector.tensor_tensor(dst, a, b, op)

            def heads(p, n, seen, is_q):
                c.step("xs", seen)
                dve.wait_ge(S("xs"), c.at("xs"))
                dve.sem_inc(S("dve_turn"), 1)
                own("rope", nc.vector.stream_shuffle(G[:, 0:LAT], XG[:, p, 0:LAT], [(k + 16) % 32 for k in range(32)]))
                tt(G[:, 0:LAT], G[:, 0:LAT], SIN, ALU.mult).then_inc(S("rope"), 1)
                tt(XG[:, p, 0:LAT], XG[:, p, 0:LAT], COS, ALU.mult).then_inc(S("rope"), 1)
                c.step("rope", 2)
                dve.wait_ge(S("rope"), c.at("rope"))
                tt(XG[:, p, 0:LAT], XG[:, p, 0:LAT], G[:, 0:LAT], ALU.add).then_inc(S("rope2"), 1)
                c.step("rope2")
                dve.wait_ge(S("rope2"), c.at("rope2"))
                c.step("rs")
                dve.wait_ge(S("rs"), c.at("rs"))
                tt(XG[:, p, 0:n], XG[:, p, 0:n], R[:, 0:n], ALU.mult).then_inc(S("y"), 1)
                c.step("y")
                dve.wait_ge(S("y"), c.at("y"))
                dve.sem_inc(S("rs_free"), 1)
                c.step("qhi")
                dve.wait_ge(S("qhi"), c.at("qhi"))
                w = 0 if is_q else 1
                tt(QK[:, w, 1, 0:n], XG[:, p, 0:n], QK[:, w, 0, 0:n].bitcast(F32), ALU.subtract).then_inc(S("qk"), 1)
                c.step("qk")
                dve.wait_ge(S("qk"), c.at("qk"))
                dve.sem_inc(S(f"xg_free{p}"), 1)

            def values():
                for a in range(2):
                    b, n = c.pair("aux")
                    c.step("aux")
                    c.step("vhi")
                    dve.wait_ge(S("vhi"), c.at("vhi"))
                    tt(VT[:, 1, 3 * a:3 * a + 3, :], v4(aux[b], 0, 3, P), VT[:, 0, 3 * a:3 * a + 3, :].bitcast(F32),
                       ALU.subtract).then_inc(S(f"aux_free{b}"), 1)
                    dve.wait_ge(S(f"aux_free{b}"), n + 2)
                    dve.sem_inc(S("vlo"), 1)
                dve.sem_inc(S("xg_free0"), 1)

            def maximum(k, k0):
                s, _ = c.pair("sc")
                n = TOK if k0 == 0 else CTX
                dve.wait_ge(S("scored"), c.at("sc") + 1)
                nc.vector.tensor_reduce(NM[:, k % 4:k % 4 + 1], sco[s][:, 0:n], AX_X, ALU.max, negate=True).then_inc(S("max"), 1)
                c.step("sc")

            def turned_lo(blk, half, k0):
                for a in range(2 if k0 == 0 else 1):
                    b, n = c.pair("aux")
                    c.step("aux")
                    c.step("pth")
                    dve.wait_ge(S("pth"), c.at("pth"))
                    kk = slice(3 * a, 3 * a + 3) if k0 == 0 else slice(4, 6)
                    m = 3 if k0 == 0 else 2
                    q = slice(half * P, half * P + P)
                    tt(PT[:, blk % 2, 1, kk, q], v4(aux[b], 0, m, P), PT[:, blk % 2, 0, kk, q].bitcast(F32),
                       ALU.subtract).then_inc(S(f"aux_free{b}"), 1)
                    dve.wait_ge(S(f"aux_free{b}"), n + 2)
                    dve.sem_inc(S("pt"), 1)

            def norm(l, k, n):
                c.step("acc", 2)
                for j in range(1, KC):
                    dve.wait_ge(S("nsq"), c.at("nsq", j + 1))
                    own("nadd", tt(MM[:, 0, 0:n], MM[:, 0, 0:n], MM[:, j, 0:n], ALU.add))
                c.step("nsq", KC)
                c.step("nrs")
                dve.wait_ge(S("nrs"), c.at("nrs"))

                def lo(j):
                    c.step("nhi")
                    dve.wait_ge(S("nhi"), c.at("nhi"))
                    tt(H[:, 1, j, 0:n], MM[:, j, 0:n], H[:, 0, j, 0:n].bitcast(F32), ALU.subtract).then_inc(S("h_ready"), 1)

                for j in range(KC):
                    tt(MM[:, j, 0:n], X[:, j, 0:n], R[:, 0:n], ALU.mult).then_inc(S("ntm"), 1)
                    if j >= 2:
                        lo(j - 2)
                lo(KC - 2)
                lo(KC - 1)

            def residual(l, j, rngs, part, final=None):
                for a, w in rngs:
                    b = wait_acc()
                    ps_ = stream_pieces(a, w)
                    for k, (s, m, st) in enumerate(ps_):
                        nc.vector.scalar_tensor_tensor(
                            X[:, j, s:s + m], acc[b][:, s - a:s - a + m], MOD[:, l, part, j, st:st + 1],
                            X[:, j, s:s + m], ALU.mult, ALU.add).then_inc(S(f"acc_free{b}" if k == len(ps_) - 1 else "xpart"), 1)

            def all_evacuated():
                for back in (1, 2):
                    b, n = c.pair("acc", -back)
                    dve.wait_ge(S(f"acc_free{b}"), n + 2)

            for p in range(2):
                dve.sem_inc(S(f"xg_free{p}"), 1)
            dve.sem_inc(S("rs_free"), 1)
            for name in ("madd", "mid_chunks", "mid_half"):
                dve.sem_inc(S(name), 1)
            dve.wait_ge(S("vecs"), 16)
            dve.wait_ge(S("consts"), 16)
            dve.wait_ge(S("wdw"), 16)
            dve.wait_ge(S("wdw_zero"), 1)
            dve.wait_ge(S("u_zero"), 1)
            for l in range(DEPTH):
                for m in range(2):
                    o = V_LAM + (l * 4 + m * 2) * HEAD
                    tt(T[:, (2 * l + m) * HEAD:(2 * l + m + 1) * HEAD], V[:, o:o + HEAD], V[:, o + HEAD:o + 2 * HEAD], ALU.mult).then_inc(S("lam_mul"), 1)
            dve.wait_ge(S("lam_mul"), 4)
            for i in range(4):
                nc.vector.tensor_reduce(LM[:, i:i + 1], T[:, i * HEAD:(i + 1) * HEAD], AX_X, ALU.add).then_inc(S("lam"), 1)
            dve.wait_ge(S("lam_exp"), 1)
            for l in range(DEPTH):
                init = 0.8 - 0.6 * math.exp(-0.3 * l)
                tt(LM[:, 12 + l:13 + l], LM[:, 9 + 2 * l:10 + 2 * l], LM[:, 8 + 2 * l:9 + 2 * l], ALU.subtract).then_inc(S("lam_sub"), 1)
                dve.wait_ge(S("lam_sub"), l + 1)
                nc.vector.tensor_scalar(NEGLAM[:, l:l + 1], LM[:, 12 + l:13 + l], -init, None, ALU.add).then_inc(S("lam_neg"), 1)
                nc.vector.tensor_scalar(GS[:, l:l + 1], V[:, V_GSUB + l:V_GSUB + l + 1], 1.0 - init, None, ALU.mult).then_inc(S("lam_neg"), 1)
            dve.wait_ge(S("mod_used"), MOD_RING + DEPTH * MOD_TILES)
            flat = "p a b c d -> p (a b c d)"
            tt(MOD[:, :, :, :, :].rearrange(flat), sco[0][:, 0:DEPTH * MOD_TILES * 2],
               V[:, V_BMOD:V_BMOD + DEPTH * MOD_TILES * 2], ALU.add).then_inc(S("mod_sum"), 1)
            dve.wait_ge(S("mod_sum"), 1)
            for l in range(DEPTH):
                for k in range(2):
                    nc.vector.scalar_tensor_tensor(
                        A[:, l, k, :, :], MOD[:, l, SC1 if k == 0 else SC2, :, :], 1.0,
                        v4(V, V_G + (2 * l + k) * KC * 2, KC, 2), ALU.add, ALU.mult).then_inc(S("mod_gain"), 1)
            dve.wait_ge(S("mod_gain"), 4)
            dve.wait_ge(S("lam_neg"), 4)
            dve.sem_inc(S("mod_ready"), 1)
            dve.wait_ge(S("x"), 16)

            for l in range(DEPTH):
                wide, slim = ranges(l, True), ranges(l, False)
                n = n_tok(l)
                norm(l, 0, TOK)
                c.step("acc", 4)
                c.step("aux", 2)
                heads(1, TOK, 2, False)
                values()
                with c.repeat(dve, 4, dict(per_gqa(l), rope2=1)) as j:
                    c.step("acc", per_gqa(l)["acc"])
                    c.step("aux", 2)
                    heads(0, n, nr(l), True)
                    items = [(hp, q, k0, hp * nb(l) + m) for hp in range(2) for q, k0, m in qtiles(l)]
                    maximum(0, items[0][2])
                    maximum(1, items[1][2])
                    for i, (hp, q, k0, blk) in enumerate(items):
                        nk = TOK if k0 == 0 else CTX
                        s = i % 4
                        ahead = min(2, len(items) - i)
                        dve.wait_ge(S("exp"), c.at("sc", 3 - ahead))
                        own("recip", nc.vector.reciprocal(RL[:, s:s + 1], L[:, s:s + 1]))
                        nc.vector.tensor_scalar(PR[:, s, 0:nk], PR[:, s, 0:nk], RL[:, s:s + 1], None, ALU.mult).then_inc(S("pn"), 1)
                        c.step("pn")
                        if i + 2 < len(items):
                            maximum(i + 2, items[i + 2][2])
                        turned_lo(blk, i % 2, k0)
                with c.repeat(dve, 4, dict(per_diff(l), rope2=2)) as h:
                    acc0 = c.n["acc"]
                    c.step("aux", 2)
                    heads(0, n, nr(l), True)
                    c.step("aux", 2)
                    heads(1, TOK, 2, False)
                    values()
                    for i, (a, w) in enumerate(slim):
                        c.step("sg")
                        dve.wait_ge(S("sg"), c.at("sg"))
                        for s, o, m in conv_pieces(a, w):
                            u = U[:, bass.ds(h * UW + (PAD + o), m)]
                            tt(u, u, XS[:, 1, s:s + m], ALU.mult).then_inc(S("glu"), 1)
                            glu_n = len(conv_pieces(a, w))
                            c.step("glu")
                    dve.wait_ge(S("glu"), c.at("glu"))
                    dve.sem_inc(S("xg_free1"), 1)
                    items = [(0, q, k0, m) for q, k0, m in qtiles(l)]
                    for k in range(2):
                        maximum(k, items[0][2])

                    def sub(w):
                        q0 = items[2 * w][1]
                        c.step("orr")
                        dve.wait_ge(S("orr"), c.at("orr"))
                        o = X[:, h + 4, q0:q0 + 256]
                        nc.vector.scalar_tensor_tensor(o, o, GS[:, l:l + 1], T[:, q0:q0 + 256], ALU.mult, ALU.mult).then_inc(S("od"), 1)

                    for i, (_, q, k0, blk) in enumerate(items):
                        nk = TOK if k0 == 0 else CTX
                        s = (2 * i) % 4
                        dve.wait_ge(S("exp"), c.at("sc", 2))
                        own("recip", nc.vector.reciprocal(RL[:, s:s + 2], L[:, s:s + 2]))
                        tt(RLN[:, i % 2:i % 2 + 1], RL[:, s + 1:s + 2], NEGLAM[:, l:l + 1], ALU.mult).then_inc(S("rl"), 1)
                        if i + 1 < len(items):
                            maximum(2 * i + 2, items[i + 1][2])
                            maximum(2 * i + 3, items[i + 1][2])
                        c.step("pb")
                        dve.wait_ge(S("pb"), c.at("pb"))
                        nc.vector.scalar_tensor_tensor(PR[:, s, 0:nk], PR[:, s, 0:nk], RL[:, s:s + 1], PR[:, s + 1, 0:nk],
                                                       ALU.mult, ALU.add).then_inc(S("pn"), 1)
                        c.step("pn")
                        turned_lo(blk, i % 2, k0)
                        if (i % 2 == 0 and i) or i == len(items) - 1:
                            w = i // 2 - 1 if i % 2 == 0 else i // 2
                            if w:
                                sub(w - 1)
                    sub(nb(l) - 1)
                    c.n["acc"] = acc0 + per_diff(l)["acc"]
                for k in range(KC):
                    c.step("bhi")
                    dve.wait_ge(S("bhi"), c.at("bhi"))
                    tt(BR[:, 1, k, 0:n], X[:, k, 0:n], BR[:, 0, k, 0:n].bitcast(F32), ALU.subtract).then_inc(S("bsplit"), 1)

                def merge(b, j):
                    c.step("acc", nr(l))
                    for a, w in slim:
                        c.step("g")
                        dve.wait_ge(S("g"), c.at("g"))
                        b_ = wait_acc()
                        if b == 0:
                            tt(MM[:, j, a:a + w], G[:, a:a + w], acc[b_][:, 0:w], ALU.mult).then_inc(S(f"acc_free{b_}"), 1)
                        else:
                            dve.wait_ge(S("madd"), c.at("madd") + 1)
                            tt(T[:, a:a + w], G[:, a:a + w], acc[b_][:, 0:w], ALU.mult).then_inc(S(f"acc_free{b_}"), 1)
                            dve.wait_ge(S(f"acc_free{b_}"), c.pair("acc", -1)[1] + 2)
                            tt(MM[:, j, a:a + w], MM[:, j, a:a + w], T[:, a:a + w], ALU.add).then_inc(S("madd"), 1)
                            c.step("madd")

                c.step("cbias", CC)
                dve.wait_ge(S("cbias"), c.at("cbias"))
                w0 = conv_width(l)
                for b in range(2):
                    pr = dict(per_merge(l), madd=nr(l) if b else 0, tap=TAPS4)
                    with c.repeat(dve, 2, {k: 4 * v for k, v in pr.items()}) as c2:
                        with c.repeat(dve, 4, pr) as q:
                            for t in range(TAPS4):
                                o = X1[:, bass.ds((c2 + 2 * b) * XW, w0)]
                                u = U[:, bass.ds((c2 + 2 * b) * UW + q * TAPS4 + t, w0)]
                                wt = WDW[:, l, :, :].rearrange("p c t -> p (c t)")[:, bass.ds((c2 + 2 * b) * 32 + q * TAPS4 + t, 1)]
                                own("tap", nc.vector.scalar_tensor_tensor(o, u, wt, o, ALU.mult, ALU.add))
                            merge(b, c2 * 4 + q)
                        for k in pr:
                            pass
                sum_ = U[:, 0:w0]
                tt(sum_, XC(l, 0), XC(l, 1), ALU.add).then_inc(S("lad"), 1)
                c.step("lad")
                for ch in (2, 3):
                    dve.wait_ge(S("lad"), c.at("lad"))
                    tt(sum_, sum_, XC(l, ch), ALU.add).then_inc(S("lad" if ch == 2 else "lsum"), 1)
                    if ch == 2:
                        c.step("lad")
                for i, (a, w) in enumerate(conv_halves(l)):
                    b_ = wait_acc()
                    for ch in range(CC):
                        o = X1[:, ch * XW + a:ch * XW + a + w]
                        ins = nc.vector.scalar_tensor_tensor(o, acc[b_][:, 0:w], -1.0 / CONV_CH, o, ALU.mult, ALU.add)
                        ins.then_inc(S(f"acc_free{b_}") if ch == CC - 1 else S("lc0"), 1)
                    dve.wait_ge(S(f"acc_free{b_}"), c.pair("acc", -1)[1] + 2)
                for ch in range(CC):
                    dve.sem_inc(S("lcen"), 1)
                c.step("acc", 2)
                for ch in range(1, CC):
                    dve.wait_ge(S("lsq"), CC * l + ch + 1)
                    ins = tt(US(l, 0), US(l, 0), US(l, ch), ALU.add)
                    if ch < CC - 1:
                        own("lad", ins)
                    else:
                        ins.then_inc(S("lsum"), 1)
                dve.wait_ge(S("lrs"), l + 1)
                for ch in range(CC):
                    tt(XC(l, ch), XC(l, ch), U[:, UW:UW + w0], ALU.mult).then_inc(S("lnx"), 1)
                for ch in range(CC):
                    for s, o, m in conv_pieces(0, n):
                        c.step("chi")
                        dve.wait_ge(S("chi"), c.at("chi"))
                        last = s + m == n
                        tt(BR[:, 1, ch, s:s + m], X1[:, ch * XW + o:ch * XW + o + m],
                           BR[:, 0, ch, s:s + m].bitcast(F32), ALU.subtract).then_inc(S("c_split" if last else "clo"), 1)
                if l == 0:
                    dve.wait_ge(S("c_split"), CC * (l + 1))
                    nc.vector.memset(U[:, :], 0.0).then_inc(S("u_zero"), 1)
                with c.repeat(dve, KC, dict(per_merge(l), madd=nr(l))) as j:
                    merge(2, j)
                dve.wait_ge(S("madd"), c.at("madd") + 1)
                dve.sem_inc(S("mdone"), 1)
                for k in range(KC):
                    c.step("mhi")
                    dve.wait_ge(S("mhi"), c.at("mhi"))
                    tt(H[:, 1, k, 0:n], MM[:, k, 0:n], H[:, 0, k, 0:n].bitcast(F32), ALU.subtract).then_inc(S("msplit"), 1)
                dve.wait_ge(S("x"), 16 * (l + 2))
                with c.repeat(dve, 4, per_out(l)) as j:
                    for s in range(2):
                        residual(l, j * 2 + s, slim, GT1)
                all_evacuated()
                dve.sem_inc(S("xres"), 1)
                norm(l, 1, n)
                for g, (k0, m) in enumerate(GROUPS):
                    with c.repeat(dve, m, per_ffn(l)) as f:
                        c.step("acc", nr(l))
                        for i, (a, w) in enumerate(slim):
                            c.step("g")
                            dve.wait_ge(S("g"), c.at("g"))
                            b_ = wait_acc()
                            name = "mid_chunks" if i == len(slim) - 1 else "mid_half"
                            dve.wait_ge(S(name), c.at(name) + 1)
                            tt(T[:, a:a + w], G[:, a:a + w], acc[b_][:, 0:w], ALU.mult).then_inc(S(f"acc_free{b_}"), 1)
                            dve.wait_ge(S(f"acc_free{b_}"), c.pair("acc", -1)[1] + 2)
                            dve.sem_inc(S("mt"), 1)
                            c.step("midh")
                            dve.wait_ge(S("midh"), c.at("midh"))
                            ins = tt(BR[:, 1, f, a:a + w], T[:, a:a + w], BR[:, 0, f, a:a + w].bitcast(F32), ALU.subtract)
                            ins.then_inc(S(name), 1)
                            c.step(name)
                    with c.repeat(dve, 4, per_out(l)) as j:
                        for s in range(2):
                            residual(l, j * 2 + s, slim, GT2)
                    all_evacuated()
                dve.sem_inc(S("x_done"), 1)


def kernel(**inputs):
    import concourse.bacc as _bacc
    from concourse.bass_utils import run_bass_kernel_spmd as _run

    a = {k: np.asarray(v) for k, v in inputs.items()}
    f32 = np.float32

    def chunks(v):
        return np.moveaxis(v.reshape(v.shape[:-1] + (-1, P)), -1, 0)

    def tiles(w):
        l, k, n = w.shape
        return np.ascontiguousarray(w.reshape(l, k // P, P, n // P, P).transpose(0, 3, 2, 1, 4).reshape(l, n // P, P, k))

    cols = lambda o: list(range(o, o + P))
    order = cols(512) + cols(640)
    for j in range(4):
        order += list(range(64 * j, 64 * j + 64)) + list(range(256 + 64 * j, 256 + 64 * j + 64)) + cols(2304 + P * j)
    for h in range(4):
        order += cols(768 + P * h) + cols(1280 + P * h) + cols(1792 + P * h) + cols(2816 + P * h)
    rows_a = [r for j in range(4) for o in (64 * j, 256 + 64 * j) for r in range(o, o + 64)]
    w_in = tiles(a["w_in"][:, :, order])
    w_br = np.concatenate([tiles(a["w_a"][:, rows_a, :]), tiles(a["w_b"]), tiles(a["w_c"])], axis=1)
    fi = tiles(a["w_ffn_in"])
    w_fi = np.ascontiguousarray(np.stack([fi[:, :FC], fi[:, FC:]], axis=2).reshape(DEPTH, 2 * FC, P, D))
    w_mod = tiles(a["w_mod"]).reshape(DEPTH * MOD_TILES, P, D)

    x_all = np.concatenate([a["x"][0], a["ctx"][0]], axis=0)
    xT = np.ascontiguousarray(x_all.T.reshape(KC, P, TOK).transpose(1, 0, 2))

    two = lambda v: np.repeat(v[..., None], 2, axis=-1).reshape(P, -1)
    heads2 = lambda v: np.concatenate([v, v], axis=-1)
    gains = np.stack([heads2(a[k]) for k in ("g_q_gqa", "g_k_gqa", "g_q_diff", "g_k_diff")], axis=1)
    lam = np.stack([a[k] for k in ("lambda_q1", "lambda_k1", "lambda_q2", "lambda_k2")], axis=1)
    vecs = np.concatenate([
        np.stack([chunks(a["c"][0]), chunks(a["c_ctx"])], axis=-1).reshape(P, -1),
        two(chunks(a["b_mod"])),
        two(chunks(np.stack([a["g_norm1"], a["g_norm2"]], axis=1))),
        chunks(a["b_gate"]).reshape(P, -1),
        gains.transpose(2, 0, 1).reshape(P, -1),
        a["g_subln"].T,
        chunks(a["b_dw"]).reshape(P, -1),
        chunks(a["g_conv_ln"]).reshape(P, -1),
        chunks(a["b_conv_ln"]).reshape(P, -1),
        np.broadcast_to(lam.reshape(1, -1), (P, lam.size)),
    ], axis=1)
    wdw = np.ascontiguousarray(a["w_dw"].reshape(DEPTH, TAPS, CC, P).transpose(3, 0, 2, 1))

    row = np.repeat(np.arange(LAT // GRID_W, dtype=f32), GRID_W)
    col = np.tile(np.arange(GRID_W, dtype=f32), LAT // GRID_W)
    inv = (f32(THETA) ** (-np.arange(16, dtype=f32) / f32(16))).astype(f32)
    feature = np.arange(P) % HEAD
    ang = np.where((feature < 32)[:, None], row[None, :], col[None, :]).astype(f32) * inv[feature % 16][:, None]
    sign = np.where(feature % 32 < 16, -1.0, 1.0).astype(f32)[:, None]
    same = np.arange(P)[:, None] // HEAD == np.arange(P)[None, :] // HEAD
    consts = np.concatenate([np.cos(ang), np.sin(ang) * sign, np.ones((P, P)), same, np.eye(P)], axis=1).astype(f32)

    nc = _bacc.Bacc("TRN2", target_bir_lowering=False, num_devices=1)
    arrays = {"xT": xT, "vecs": np.ascontiguousarray(vecs), "consts": consts, "wdw": wdw, "w_mod": w_mod, "w_in": w_in,
              "w_gate": tiles(a["w_gate"]), "w_br": np.ascontiguousarray(w_br), "w_out": tiles(a["w_out"]),
              "w_fi": w_fi, "w_fo": tiles(a["w_ffn_out"])}
    ins = {k: nc.dram_tensor("in_" + k, v.shape, F32, kind="ExternalInput").ap() for k, v in arrays.items()}
    out = nc.dram_tensor("out_x", (P, KC, LAT), F32, kind="ExternalOutput").ap()
    build(nc, out=out, **ins)
    r = _run(nc, [{"in_" + k: v for k, v in arrays.items()}], core_ids=[0])
    y = r.results[0]["out_x"]
    return np.ascontiguousarray(y.transpose(1, 0, 2).reshape(D, LAT).T).reshape(1, LAT, D)
```

```python
from contextlib import ExitStack, contextmanager
import math

import numpy as np
import concourse.bass as bass
from concourse import mybir

F32 = mybir.dt.float32
F32R = mybir.dt.float32r
ALU = mybir.AluOpType
ACT = mybir.ActivationFunctionType
AX_X = mybir.AxisListType.X

P = 128
D = 1024
KC = D // P
DEPTH = 2
LAT, CTX = 512, 256
TOK = LAT + CTX
HEAD = 64
GRID_W = 64
THETA = 10000.0
EPS = 1e-6
CONV_CH, TAPS = 512, 31
CC = CONV_CH // P
PAD = TAPS // 2
TAPS4 = 8
UW = PAD + LAT + PAD + CTX + PAD + 1
D_FF = 2816
FC = D_FF // P
IN_TILES = 26
GROUPS = [(0, 8), (8, 8), (16, 6)]
MOD_GROUP = 256
MOD_GROUPS = 6 * D // MOD_GROUP
MOD_FIRST = 2 * D // MOD_GROUP
SH1, SC1, GT1, SH2, SC2, GT2 = range(6)

V_C = 0
V_BMOD = V_C + KC * 2
V_G = V_BMOD + DEPTH * 6 * KC * 2
V_BGATE = V_G + DEPTH * 2 * KC * 2
V_GQK = V_BGATE + DEPTH * 24
V_GSUB = V_GQK + DEPTH * 4
V_BDW = V_GSUB + DEPTH
V_GLN = V_BDW + DEPTH * CC
V_BLN = V_GLN + DEPTH * CC
V_LAM = V_BLN + DEPTH * CC
VECS = V_LAM + DEPTH * 4 * HEAD
K_COS, K_SIN, K_ONES, K_BLOCK, K_ID = 0, LAT, 2 * LAT, 2 * LAT + P, 2 * LAT + 2 * P
CONSTS = 2 * LAT + 3 * P


class Counts:

    def __init__(self):
        self.n, self.loops = {}, []

    def at(self, name, off=0):
        v = self.n.get(name, 0) + off
        for i, per in self.loops:
            if per.get(name):
                v = i * per[name] + v
        return v

    def pair(self, name, off=0):
        k = self.n.get(name, 0) + off
        v = k // 2
        for i, per in self.loops:
            assert per.get(name, 0) % 2 == 0, name
            if per.get(name):
                v = i * (per[name] // 2) + v
        return k % 2, v

    def step(self, name, k=1):
        self.n[name] = self.n.get(name, 0) + k

    @contextmanager
    def repeat(self, eng, n, per):
        before = dict(self.n)
        with eng.Fori(0, n) as i:
            self.loops.append((i, per))
            yield i
            self.loops.pop()
        for name in set(self.n) | set(per):
            moved = self.n.get(name, 0) - before.get(name, 0)
            assert moved in (0, per.get(name, 0)), (name, moved, per.get(name, 0))
            self.n[name] = before.get(name, 0) + n * per.get(name, 0)


def stream_pieces(a, n):
    if a < LAT < a + n:
        return [(a, LAT - a, 0), (LAT, a + n - LAT, 1)]
    return [(a, n, 0 if a < LAT else 1)]


def build(nc, xT, vecs, consts, wdw, w_mod, w_in, w_gate, w_br, w_out, w_fi, w_fo, out):
    x_next = nc.dram_tensor("x_next", (P, KC, LAT), F32).ap()

    with ExitStack() as ctx:
        def sb(name, shape, dt):
            return ctx.enter_context(nc.sbuf_tensor(name, shape, dt))

        sems = {}

        def S(name):
            if name not in sems:
                sems[name] = ctx.enter_context(nc.semaphore("s_" + name))
            return sems[name]

        H = sb("H", [P, 2, KC, TOK], F32R)
        RB = sb("RB", [P, 2 * KC * TOK], F32R)
        WHI = sb("WHI", [P, 2, KC * P], F32R)
        WLO = sb("WLO", [P, 2, KC * P], F32R)
        STG = sb("STG", [P, 2, KC * P], F32)
        X = sb("X", [P, KC, TOK], F32)
        M = sb("M", [P, KC * TOK + 768], F32)
        U = sb("U", [P, CC * UW], F32)
        G = sb("G", [P, TOK], F32)
        T = sb("T", [P, TOK], F32)
        R = sb("R", [P, TOK], F32)
        V = sb("V", [P, VECS], F32)
        K = sb("K", [P, CONSTS], F32)
        WDW = sb("WDW", [P, DEPTH, CC, 4 * TAPS4], F32)
        MOD = sb("MOD", [P, DEPTH, 6, KC, 2], F32)
        A = sb("A", [P, DEPTH, 2, KC, 2], F32)
        SCX = sb("SCX", [P, KC, P], F32R)

        NEGLAM = sb("NEGLAM", [P, DEPTH], F32)
        GS = sb("GS", [P, DEPTH], F32)
        EC = sb("EC", [P, 4], F32)
        NM = sb("NM", [P, 4], F32)
        L = sb("L", [P, 4], F32)
        RL = sb("RL", [P, 4], F32)
        RLN = sb("RLN", [P, 2], F32)

        v4 = lambda t, o, a, b: t[:, o:o + a * b].rearrange("p (a b) -> p a b", b=b)
        cat = lambda t, k, n=TOK: v4(t, k * n, 1, n)[:, 0, :]
        QK = RB[:, 0:4 * TOK].rearrange("p (w s t) -> p w s t", w=2, s=2)
        VT = RB[:, 4 * TOK:6 * TOK].rearrange("p (s k d) -> p s k d", s=2, k=6)
        PT = RB[:, 6 * TOK:6 * TOK + 4 * 1536].rearrange("p (b s k q) -> p b s k q", b=2, s=2, k=6)
        BR = RB[:, :].rearrange("p (s k t) -> p s k t", s=2, k=KC)
        MOD1 = MOD[:, :, :, :, :].rearrange("p l a k s -> p (l a k s)")
        MM = M[:, 0:KC * TOK].rearrange("p (k t) -> p k t", k=KC)
        PR = M[:, 0:4 * TOK].rearrange("p (n t) -> p n t", n=4)
        XG = M[:, 4 * TOK:6 * TOK].rearrange("p (n t) -> p n t", n=2)
        XS = M[:, 6 * TOK:8 * TOK].rearrange("p (n t) -> p n t", n=2)
        OSQ = M[:, 8 * TOK:9 * TOK].rearrange("p (n q) -> p n q", n=3)
        MROW = M[0:4, 8 * TOK:8 * TOK + MOD_GROUP]
        SC = v4(R, 0, KC, 2)
        LM = R[:, 16:32]
        COS, SIN = K[:, K_COS:K_COS + LAT], K[:, K_SIN:K_SIN + LAT]
        ONES, BLOCK, IDENT = (K[:, o:o + P] for o in (K_ONES, K_BLOCK, K_ID))

        ps = lambda n, w: ctx.enter_context(nc.psum_tensor(n, [P, w], F32))
        acc = [ps("acc0", 512), ps("acc1", 512)]
        aux = [ps("aux0", 512), ps("aux1", 512)]
        sco = [ps("sco0", 1024), ps("sco1", 1024)]

        def n_tok(l):
            return TOK if l == 0 else LAT

        def ranges(l, wide):
            if l == 0:
                return [(0, 384), (384, 384)]
            return [(0, LAT), (LAT, CTX)] if wide else [(0, LAT)]

        def blocks(l):
            return [(0, 0), (256, 0)] + ([(LAT, 4)] if l == 0 else [])

        def qtiles(l):
            return [(q, k0, n) for n, (c0, k0) in enumerate(blocks(l)) for q in (c0, c0 + 128)]

        def halves(n):
            return [(0, n // 2), (n // 2, n // 2)]

        nr = lambda l: len(ranges(l, False))
        nb = lambda l: len(blocks(l))
        aux_att = lambda l: sum(2 if k0 == 0 else 1 for _, k0, _ in qtiles(l))

        def per_gqa(l):
            return dict(tile=2, acc=2 * nr(l) + 2 * nb(l), aux=2 + 2 * aux_att(l),
                        rs=1, y=1, qk=1, rope=3, rope2=1, qhi=1,
                        sc=4 * nb(l), pn=4 * nb(l), pth=2 * aux_att(l), recip=4 * nb(l))

        def per_diff(l):
            return dict(tile=4, acc=2 * nr(l) + 4 + 2 * nb(l), aux=2 + 2 + 2 + aux_att(l),
                        rs=2, y=2, qk=2, rope=6, rope2=2, qhi=2,
                        sc=4 * nb(l), pn=2 * nb(l), rl=2 * nb(l), pb=2 * nb(l),
                        pth=aux_att(l), recip=2 * nb(l), vhi=2, glu=sum(len(stream_pieces(a, w)) for a, w in ranges(l, False)), orr=nb(l))

        def mod_here(l, b=None, g=None):
            return l == 0 and (b is not None or g < 2)

        def with_mod(per, here):
            return dict(per, tile=per["tile"] + 2, mod=1) if here else per

        def per_merge(l, b):
            return with_mod(dict(tile=2, acc=2 * nr(l)), mod_here(l, b=b))

        def per_out(l):
            return dict(tile=2, acc=2 * nr(l))

        def per_ffn(l, g):
            return with_mod(dict(tile=2, acc=2 * nr(l), midh=nr(l), mid_chunks=1, mid_half=nr(l) - 1),
                            mod_here(l, g=g))

        def wait_read(eng, c, kind, *backs):
            for back in backs:
                b, n = c.pair(kind, -back)
                eng.wait_ge(S(f"{kind}_free{b}"), n + 2)

        def conv_width(l):
            return UW - TAPS if l == 0 else LAT

        def conv_halves(l):
            w = conv_width(l)
            return [(0, w // 2 + w % 2), (w // 2 + w % 2, w // 2)]

        def conv_pieces(a, n):
            return [(s, s if t == 0 else s + PAD, w) for s, w, t in stream_pieces(a, n)]

        XW = UW - TAPS
        X1 = X[:, :, :].rearrange("p k t -> p (k t)")

        def XC(l, ch):
            return X1[:, ch * XW:ch * XW + conv_width(l)]

        def US(l, ch):
            return U[:, ch * UW:ch * UW + conv_width(l)]

        block = ctx.enter_context(nc.Block())

        @block.sync
        def _(sp):
            c = Counts()

            def tile(src, n):
                s, _ = c.pair("tile")
                dst = STG[:, s, 0:n]
                sp.wait_ge(S("w_split"), 2 * c.at("tile") + 2)
                sp.dma_start(dst, src).then_inc(S(f"w_load{s}"), 16)
                c.step("tile")

            sp.dma_start(V[:, :], vecs).then_inc(S("vecs"), 16)
            sp.dma_start(K[:, :], consts).then_inc(S("consts"), 16)
            sp.dma_start(WDW[:, :, :, 0:TAPS], wdw).then_inc(S("wdw"), 16)
            sp.dma_start(X[:, :, :], xT).then_inc(S("x"), 16)
            with c.repeat(sp, MOD_FIRST, dict(tile=2)) as i:
                for q in range(2):
                    tile(w_mod[i, q], KC * P)
            for l in range(DEPTH):
                tile(w_in[l, 0], KC * P)
                tile(w_in[l, 1], KC * P)
                with c.repeat(sp, 4, per_gqa(l)) as j:
                    for s in range(2):
                        tile(w_in[l, j * 2 + (2 + s)], KC * P)
                with c.repeat(sp, 4, per_diff(l)) as h:
                    for s in range(4):
                        tile(w_in[l, h * 4 + (10 + s)], KC * P)
                for b in range(3):
                    with c.repeat(sp, KC, per_merge(l, b)) as j:
                        if mod_here(l, b=b):
                            tile(w_mod[j + (MOD_FIRST + b * KC), 0], KC * P)
                        tile(w_gate[l, j + b * KC], KC * P)
                        if mod_here(l, b=b):
                            tile(w_mod[j + (MOD_FIRST + b * KC), 1], KC * P)
                        tile(w_br[l, j + b * KC], CC * P)
                    if b == 2:
                        sp.wait_ge(S("c_split"), CC * (l + 1))
                        if l == 0:
                            sp.dma_start(X[:, :, :], xT).then_inc(S("x"), 16)
                        else:
                            sp.dma_start(X[:, :, 0:LAT], x_next).then_inc(S("x"), 16)
                with c.repeat(sp, 4, per_out(l)) as j:
                    for s in range(2):
                        tile(w_out[l, j * 2 + s], KC * P)
                for g, (k0, n) in enumerate(GROUPS):
                    with c.repeat(sp, n, per_ffn(l, g)) as f:
                        for s in range(2):
                            if mod_here(l, g=g):
                                tile(w_mod[f + (MOD_GROUPS + (g + 1) * KC), s], KC * P)
                            tile(w_fi[l, f * 2 + (2 * k0 + s)], KC * P)
                    with c.repeat(sp, 4, per_out(l)) as j:
                        for s in range(2):
                            tile(w_fo[l, j * 2 + s][:, k0 * P:(k0 + n) * P], n * P)
                sp.wait_ge(S("x_done"), l + 1)
                if l == 0:
                    sp.dma_start(x_next, X[:, :, 0:LAT]).then_inc(S("saved"), 16)
                    sp.wait_ge(S("saved"), 16)
                    sp.sem_inc(S("x_saved"), 1)
                else:
                    sp.dma_start(out, X[:, :, 0:LAT]).then_inc(S("stored"), 16)
                    sp.wait_ge(S("stored"), 16)

        @block.gpsimd
        def _(pool):
            c = Counts()

            def split(n):
                s, _ = c.pair("tile")
                for h, (a, w) in enumerate(halves(n)):
                    pool.wait_ge(S("w_hi"), 2 * c.at("tile") + h + 1)
                    nc.gpsimd.tensor_tensor(WLO[:, s, a:a + w], STG[:, s, a:a + w], WHI[:, s, a:a + w].bitcast(F32),
                                            ALU.subtract).then_inc(S("w_split"), 1)
                c.step("tile")

            pool.sem_inc(S("w_split"), 4)
            nc.gpsimd.memset(U[:, :], 0.0).then_inc(S("u_zero"), 1)
            nc.gpsimd.memset(EC[:, 0:1], EPS).then_inc(S("ec"), 1)
            nc.gpsimd.memset(EC[:, 1:2], HEAD * EPS).then_inc(S("ec"), 1)
            nc.gpsimd.memset(EC[:, 2:3], 0.0).then_inc(S("ec"), 1)
            nc.gpsimd.memset(WDW[:, :, :, TAPS:4 * TAPS4], 0.0).then_inc(S("wdw_zero"), 1)
            nc.gpsimd.memset(SCX[:, :, :].bitcast(F32), 0.0).then_inc(S("scx_zero"), 1)
            nc.gpsimd.memset(T[:, :], 0.0).then_inc(S("t_zero"), 1)
            with c.repeat(pool, MOD_FIRST, dict(tile=2)):
                split(KC * P)
                split(KC * P)
            for l in range(DEPTH):
                split(KC * P)
                split(KC * P)
                with c.repeat(pool, 4, per_gqa(l)):
                    for s in range(2):
                        split(KC * P)
                with c.repeat(pool, 4, per_diff(l)):
                    for s in range(4):
                        split(KC * P)
                for b in range(3):
                    with c.repeat(pool, KC, per_merge(l, b)):
                        for m in ([KC, KC, KC, CC] if mod_here(l, b=b) else [KC, CC]):
                            split(m * P)
                with c.repeat(pool, 4, per_out(l)):
                    for s in range(2):
                        split(KC * P)
                for g, (k0, n) in enumerate(GROUPS):
                    with c.repeat(pool, n, per_ffn(l, g)):
                        if mod_here(l, g=g):
                            split(KC * P)
                            split(KC * P)
                        for s in range(2):
                            split(KC * P)
                    with c.repeat(pool, 4, per_out(l)):
                        for s in range(2):
                            split(n * P)

        @block.tensor
        def _(pe):
            c = Counts()

            def open_acc():
                b, n = c.pair("acc")
                pe.wait_ge(S(f"acc_free{b}"), n + 1)
                return acc[b]

            def close_acc(mm):
                mm.then_inc(S("acc_full"), 1)
                c.step("acc")

            def open_aux():
                b, n = c.pair("aux")
                pe.wait_ge(S(f"aux_free{b}"), n + 1)
                return aux[b]

            def close_aux(mm):
                mm.then_inc(S("aux_full"), 1)
                c.step("aux")

            def product(dst, lh, ll, rh, rl, first, last):
                nc.tensor.matmul(dst, lh, rh, start=first, stop=False)
                nc.tensor.matmul(dst, lh, rl, start=False, stop=False)
                return nc.tensor.matmul(dst, ll, rh, start=False, stop=last)

            def wait_half(h):
                pe.wait_ge(S("w_split"), 2 * c.at("tile") + (h + 5))

            def tile(kn, moving, rngs, ready=None, between=None):
                s, _ = c.pair("tile")
                for n, (a, w) in enumerate(rngs):
                    dst = open_acc()
                    for k in range(kn):
                        if n == 0 and k in (0, kn // 2):
                            wait_half(k // (kn // 2))
                        if ready and n == 0:
                            pe.wait_ge(S(ready[0]), ready[1] + k + 1)
                        if between and n == len(rngs) - 1 and k == kn // 2:
                            between()
                        mm = product(dst[:, 0:w], WHI[:, s, k * P:(k + 1) * P], WLO[:, s, k * P:(k + 1) * P],
                                     moving[:, 0, k, a:a + w], moving[:, 1, k, a:a + w], k == 0, k == kn - 1)
                    close_acc(mm)
                c.step("tile")

            def mod_half(q):
                if q == 0:
                    pe.wait_ge(S("mod_row"), c.at("mod") + 1)
                s, _ = c.pair("tile")
                for k in range(4):
                    if k % 2 == 0:
                        wait_half(k // 2)
                    for w in (WHI, WLO):
                        mm = nc.tensor.matmul(sco[0][:, 0:MOD_GROUP], SCX[:, 4 * q + k, :],
                                              w[:, s, k * MOD_GROUP:(k + 1) * MOD_GROUP],
                                              start=(q == k == 0 and w is WHI), stop=(q == 1 and k == 3 and w is WLO))
                mm.then_inc(S("mod_full"), 1)
                c.step("tile")
                c.step("mod", q)

            def turn_mod():
                pe.wait_ge(S("mod_row"), c.at("mod") + 1)
                pe.wait_ge(S("mod_sum"), c.at("mod"))
                pe.sem_inc(S("pe_turn"), 1)
                for k in range(2):
                    t = nc.tensor.transpose(sco[1][:, 4 * k:4 * k + 4], MROW[:, k * P:(k + 1) * P], IDENT[0:4, 0:4])
                t.then_inc(S("mod_turned"), 1)

            def head_sums(p, n, *backs):
                wait_read(pe, c, "acc", *backs)
                for a, w in halves(n):
                    close_aux(nc.tensor.matmul(open_aux()[:, 0:w], BLOCK, XS[:, p, a:a + w], start=True, stop=True))

            def turn_v(p, *backs):
                wait_read(pe, c, "acc", *backs)
                for a in range(2):
                    dst = open_aux()
                    for k in range(3):
                        t = nc.tensor.transpose(dst[:, k * P:(k + 1) * P], XG[:, p, (3 * a + k) * P:(3 * a + k + 1) * P], IDENT)
                    close_aux(t)

            def score(side, q, k0):
                s, n = c.pair("sc")
                pe.wait_ge(S("exp"), c.at("sc") + 1)
                h = slice(side * HEAD, side * HEAD + HEAD)
                for a, w, o in ([(0, LAT, 0), (LAT, CTX, LAT)] if k0 == 0 else [(LAT, CTX, 0)]):
                    mm = product(sco[s][:, o:o + w], QK[h, 0, 0, q:q + P], QK[h, 0, 1, q:q + P],
                                 QK[h, 1, 0, a:a + w], QK[h, 1, 1, a:a + w], True, True)
                mm.then_inc(S("scored"), 1)
                c.step("sc")

            def turn_probs(slot, k0):
                c.step("pn")
                pe.wait_ge(S("pn"), c.at("pn"))
                ks = list(range(k0, 6))
                for part in ([ks[0:3], ks[3:6]] if k0 == 0 else [ks]):
                    dst = open_aux()
                    for n, k in enumerate(part):
                        t = nc.tensor.transpose(dst[:, n * P:(n + 1) * P], PR[:, slot, (k - k0) * P:(k - k0 + 1) * P], IDENT)
                    close_aux(t)

            def weigh(blk, k0, since):
                wait_read(pe, c, "aux", since + 1, since + 2)
                dst = open_acc()
                for k in range(k0, 6):
                    mm = product(dst[:, 0:256], VT[:, 0, k, :], VT[:, 1, k, :],
                                 PT[:, blk % 2, 0, k, :], PT[:, blk % 2, 1, k, :], k == k0, k == 5)
                close_acc(mm)

            def sub_sums(blk):
                wait_read(pe, c, "acc", 1)
                close_acc(nc.tensor.matmul(open_acc()[:, 0:256], ONES, OSQ[:, blk % 3, :], start=True, stop=True))

            def norm_sums(n, src):
                for a, w in halves(n):
                    close_acc(nc.tensor.matmul(open_acc()[:, 0:w], ONES, src[:, a:a + w], start=True, stop=True))

            def norm(l, k, n):
                c.step("nadd", KC if (l, k) == (0, 0) else KC - 1)
                pe.wait_ge(S("nadd"), c.at("nadd"))
                norm_sums(n, T if (l, k) == (0, 0) else MM[:, 0, :])

            def attention_items(l, maps):
                if maps == 1:
                    return [(hp, q, k0, hp * nb(l) + n) for hp in range(2) for q, k0, n in qtiles(l)]
                return [(0, q, k0, n) for q, k0, n in qtiles(l)]

            pe.wait_ge(S("consts"), 16)
            pe.wait_ge(S("scx"), 1)
            with c.repeat(pe, MOD_FIRST, dict(tile=2, mod=1)):
                mod_half(0)
                mod_half(1)
                turn_mod()
            for l in range(DEPTH):
                norm(l, 0, TOK)
                wide, slim = ranges(l, True), ranges(l, False)
                n = n_tok(l)
                tile(KC, H, wide, ready=("h_ready", 2 * KC * l))
                tile(KC, H, wide, between=lambda: head_sums(1, TOK, 2, 3))
                turn_v(0, 1, 2)
                for maps, per in ((1, per_gqa(l)), (2, per_diff(l))):
                    if maps == 1:
                        c.step("qk", 1)
                    with c.repeat(pe, 4, per):
                        if maps == 1:
                            tile(KC, H, slim)
                            tile(KC, H, slim, between=lambda: head_sums(0, n, *range(nr(l), 2 * nr(l))))
                            c.step("qk", 1)
                        else:
                            tile(KC, H, slim)
                            tile(KC, H, wide, between=lambda: head_sums(0, n, *range(2, 2 + nr(l))))
                            tile(KC, H, wide, between=lambda: head_sums(1, TOK, 2, 3))
                            tile(KC, H, slim, between=lambda: turn_v(0, nr(l), nr(l) + 1))
                            c.step("qk", 2)
                        pe.wait_ge(S("qk"), c.at("qk"))
                        if maps == 2:
                            wait_read(pe, c, "aux", 1, 2)
                        items = attention_items(l, maps)
                        ahead = 2 if maps == 1 else 1

                        def scores(i):
                            side, q, k0, _ = items[i]
                            for m in range(maps):
                                score(side if maps == 1 else m, q, k0)

                        done = 0
                        for i in range(ahead):
                            scores(i)
                        for i, (side, q, k0, blk) in enumerate(items):
                            if i + ahead < len(items):
                                scores(i + ahead)
                            turn_probs((i * maps) % 4, k0)
                            if (i % 2 == 0 and i) or i == len(items) - 1:
                                for blk in ([i // 2 - 1] if i % 2 == 0 else [i // 2]):
                                    k0 = items[2 * blk][2]
                                    if maps == 2 and blk:
                                        sub_sums(blk - 1)
                                    since = 0 if i % 2 else (2 if items[i][2] == 0 else 1)
                                    weigh(blk, k0, since)
                        if maps == 2:
                            sub_sums(nb(l) - 1)
                for b in range(3):
                    for j in range(1):
                        with c.repeat(pe, KC, per_merge(l, b)):
                            if mod_here(l, b=b):
                                mod_half(0)
                            tile(KC, H, slim)
                            if mod_here(l, b=b):
                                mod_half(1)
                            tile(CC, BR[:, :, 4 * (b % 2):4 * (b % 2) + 4, :], slim,
                                 ready=(("bsplit", 8 * l + 4 * b) if b < 2 else ("c_split", CC * l)),
                                 between=turn_mod if mod_here(l, b=b) else None)
                    if b == 1:
                        w = LAT if l == 0 else LAT // 2
                        for k in range(2):
                            c.step("lsum")
                            pe.wait_ge(S("lsum"), c.at("lsum"))
                            for a, w in conv_halves(l):
                                close_acc(nc.tensor.matmul(open_acc()[:, 0:w], ONES, U[:, a:a + w], start=True, stop=True))
                with c.repeat(pe, 4, per_out(l)):
                    for s in range(2):
                        tile(KC, H, slim, ready=("msplit", KC * l))
                norm(l, 1, n)
                for g, (k0, m) in enumerate(GROUPS):
                    with c.repeat(pe, m, per_ffn(l, g)):
                        for s in range(2):
                            if mod_here(l, g=g):
                                mod_half(s)
                            tile(KC, H, slim, ready=(("h_ready", 2 * KC * l + KC) if s == 0 and g == 0 else None),
                                 between=turn_mod if s == 1 and mod_here(l, g=g) else None)
                    with c.repeat(pe, 4, per_out(l)):
                        for s in range(2):
                            tile(m, BR, slim, ready=("mid_chunks", 1 + FC * l + k0) if s == 0 else None)

        @block.scalar
        def _(act):
            c = Counts()

            def wait_acc():
                b, n = c.pair("acc")
                act.wait_ge(S("acc_full"), c.at("acc") + 2)
                c.step("acc")
                return b

            def wait_aux():
                b, n = c.pair("aux")
                act.wait_ge(S("aux_full"), c.at("aux") + 1)
                c.step("aux")
                return b

            def settle():
                act.sem_inc(S("act_turn"), 1)

            def hi(n=KC * P, acc=0, modt=0):
                s, k = c.pair("tile")
                act.wait_ge(S(f"w_load{s}"), k * 16 + 16)
                act.wait_ge(S("acc_full"), c.at("acc") + (acc + 1))
                act.wait_ge(S("mod_full"), c.at("modt") + (modt + 1))
                for a, w in halves(n):
                    nc.scalar.activation(WHI[:, s, a:a + w], STG[:, s, a:a + w], ACT.Copy).then_inc(S("w_hi"), 1)
                c.step("tile")

            def fn(dst, src, f, sem=None, **kw):
                ins = nc.scalar.activation(dst, src, f, **kw)
                if sem:
                    ins.then_inc(S(sem), 1)
                return ins

            def exp_set():
                nc.scalar.preload_act_table_set("natural_log_exp_and_others")

            def evac_norm(l, p, rngs, g):
                for a, w in rngs:
                    b = wait_acc()
                    fn(XG[:, p, a:a + w], acc[b][:, 0:w], ACT.Identity, scale=V[:, V_GQK + 4 * l + g:V_GQK + 4 * l + g + 1], bias=EC[:, 2:3], sem="xgw")
                    fn(XS[:, p, a:a + w], acc[b][:, 0:w], ACT.Square, sem=f"acc_free{b}")

            def finish_norm(p, n, is_q):
                for a, w in halves(n):
                    b = wait_aux()
                    fn(R[:, a:a + w], aux[b][:, 0:w], ACT.Ln, scale=1.0 if is_q else 1.0 / HEAD,
                       bias=EC[:, 1:2] if is_q else EC[:, 0:1], sem=f"aux_free{b}")
                    act.wait_ge(S(f"aux_free{b}"), c.pair("aux", -1)[1] + 2)
                fn(R[:, 0:n], R[:, 0:n], ACT.Exp, scale=-0.5, sem="rs")
                c.step("rs")
                c.step("y")
                act.wait_ge(S("y"), c.at("y"))
                fn(QK[:, 0 if is_q else 1, 0, 0:n], XG[:, p, 0:n], ACT.Copy, sem="qhi")
                c.step("qk")

            def evac_v(p, rngs):
                for a, w in rngs:
                    b = wait_acc()
                    fn(XG[:, p, a:a + w], acc[b][:, 0:w], ACT.Copy, sem=f"acc_free{b}")

            def finish_v():
                for a in range(2):
                    b = wait_aux()
                    fn(VT[:, 0, 3 * a:3 * a + 3, :], v4(aux[b], 0, 3, P), ACT.Copy, sem="vhi")

            def evac_conv_a(l, ch, rngs):
                act.wait_ge(S("u_zero"), l + 1)
                for a, w in rngs:
                    b = wait_acc()
                    ps_ = conv_pieces(a, w)
                    for k, (s, o, m) in enumerate(ps_):
                        settle()
                        fn(U[:, bass.ds(ch * UW + (PAD + o), m)], acc[b][:, s - a:s - a + m], ACT.Copy,
                           sem=f"acc_free{b}" if k == len(ps_) - 1 else "ua")

            def evac_conv_g(p, rngs):
                for a, w in rngs:
                    b = wait_acc()
                    fn(XS[:, p, a:a + w], acc[b][:, 0:w], ACT.Sigmoid, sem=f"acc_free{b}")

            def exp(k, k0):
                s, _ = c.pair("sc")
                slot = k % 4
                n = TOK if k0 == 0 else CTX
                act.wait_ge(S("max"), c.at("sc") + 1)
                fn(PR[:, slot, 0:n], sco[s][:, 0:n], ACT.Exp, bias=NM[:, slot:slot + 1], accum_out=L[:, slot:slot + 1], sem="exp")
                c.step("sc")

            def turned_hi(blk, half, k0):
                for a in range(2 if k0 == 0 else 1):
                    b = wait_aux()
                    kk = slice(3 * a, 3 * a + 3) if k0 == 0 else slice(4, 6)
                    m = 3 if k0 == 0 else 2
                    fn(PT[:, blk % 2, 0, kk, half * P:half * P + P], v4(aux[b], 0, m, P), ACT.Copy, sem="pth")

            def mod_row():
                act.wait_ge(S("mod_turned"), c.at("mod") + 1)
                act.wait_ge(S("mod_full"), c.at("modt", 2) + 1)
                fn(MROW, sco[0][0:4, 0:MOD_GROUP], ACT.Copy, sem="mod_row")
                c.step("mod")
                c.step("modt", 2)

            def per_merge_act(l, b):
                return dict(per_merge(l, b), modt=2 * mod_here(l, b=b))

            def norm(l, k, n):
                exp_set()
                if (l, k) != (0, 0):
                    for j in range(KC):
                        fn(MM[:, j, 0:n], X[:, j, 0:n], ACT.Square, sem="nsq")
                for i, (a, w) in enumerate(halves(n)):
                    b = wait_acc()
                    fn(R[:, a:a + w], acc[b][:, 0:w], ACT.Ln, scale=1.0 / D, bias=EC[:, 0:1], sem=f"acc_free{b}")
                    act.wait_ge(S(f"acc_free{b}"), c.pair("acc", -1)[1] + 2)
                fn(R[:, 0:n], R[:, 0:n], ACT.Exp, scale=-0.5, sem="nrs")
                for j in range(KC):
                    c.step("ntm")
                    act.wait_ge(S("ntm"), c.at("ntm"))
                    for a, w, s in stream_pieces(0, n):
                        sh = MOD[:, l, SH1 if k == 0 else SH2, j, s:s + 1]
                        fn(MM[:, j, a:a + w], MM[:, j, a:a + w], ACT.Identity, scale=A[:, l, k, j, s:s + 1], bias=sh, sem="naf")
                        c.step("naf")
                    act.wait_ge(S("naf"), c.at("naf"))
                    fn(H[:, 0, j, 0:n], MM[:, j, 0:n], ACT.Copy, sem="nhi")

            act.sem_inc(S("exp"), 2)
            act.sem_inc(S("acc_free0"), 1)
            act.sem_inc(S("acc_free1"), 1)
            act.sem_inc(S("aux_free0"), 1)
            act.sem_inc(S("aux_free1"), 1)
            act.wait_ge(S("vecs"), 16)
            act.wait_ge(S("ec"), 3)
            act.sem_inc(S("mod_row"), 1)
            act.sem_inc(S("acc_full"), 1)
            act.sem_inc(S("mod_full"), 1)
            act.sem_inc(S("mod_turned"), 1)
            fn(SC[:, :, :], v4(V, V_C, KC, 2), ACT.Silu, sem="silu_c")
            act.wait_ge(S("silu_c"), 1)
            act.wait_ge(S("scx_zero"), 1)
            fn(SCX[:, :, 0:2], SC[:, :, :], ACT.Copy, sem="scx_hi")
            exp_set()
            c.step("lam", 2)
            act.wait_ge(S("lam"), 4)
            fn(LM[:, 8:12], LM[:, 0:4], ACT.Exp, sem="lam_exp")
            act.wait_ge(S("x"), 16)
            hi()
            with c.repeat(act, MOD_FIRST, dict(tile=2, mod=1, modt=2)) as i:
                hi()
                fn(MM[:, i, :], X[:, i, :], ACT.Square, sem="nsq")
                hi(modt=1)
                mod_row()
            for l in range(DEPTH):
                wide, slim = ranges(l, True), ranges(l, False)
                n = n_tok(l)
                if l:
                    act.wait_ge(S("x_done"), l)
                norm(l, 0, TOK)
                hi()
                if l:
                    act.wait_ge(S("glu"), c.at("glu") + 1)
                evac_norm(l, 1, wide, 1)
                hi()
                evac_v(0, wide)
                finish_norm(1, TOK, False)
                finish_v()
                if l:
                    act.wait_ge(S("x_saved"), l)
                with c.repeat(act, 4, per_gqa(l)) as j:
                    hi()
                    act.wait_ge(S("qk"), c.at("qk"))
                    evac_norm(l, 0, slim, 0)
                    hi()
                    finish_norm(0, n, True)
                    evac_conv_a(l, j, slim)
                    items = [(hp, q, k0, hp * nb(l) + m) for hp in range(2) for q, k0, m in qtiles(l)]
                    exp(0, items[0][2])
                    for i, (hp, q, k0, blk) in enumerate(items):
                        if i + 1 < len(items):
                            exp(i + 1, items[i + 1][2])
                        turned_hi(blk, i % 2, k0)
                        if (i % 2 == 0 and i) or i == len(items) - 1:
                            w = i // 2 - 1 if i % 2 == 0 else i // 2
                            side, q0 = items[2 * w][0], items[2 * w][1]
                            b = wait_acc()
                            rows = slice(side * HEAD, side * HEAD + HEAD)
                            settle()
                            fn(X[rows, j, q0:q0 + 256], acc[b][rows, 0:256], ACT.Copy, sem=f"acc_free{b}")
                with c.repeat(act, 4, per_diff(l)) as h:
                    hi()
                    act.wait_ge(S("qk"), c.at("qk"))
                    evac_norm(l, 0, slim, 2)
                    hi()
                    act.wait_ge(S("glu"), c.at("glu") + 1)
                    c.step("glu", per_diff(l)["glu"])
                    evac_norm(l, 1, wide, 3)
                    finish_norm(0, n, True)
                    hi()
                    act.wait_ge(S("qk"), c.at("qk"))
                    evac_v(0, wide)
                    finish_norm(1, TOK, False)
                    hi()
                    finish_v()
                    act.wait_ge(S("qk"), c.at("qk"))
                    evac_conv_g(1, slim)
                    exp_set()
                    items = [(0, q, k0, m) for q, k0, m in qtiles(l)]
                    exp(0, items[0][2])
                    exp(1, items[0][2])

                    def sub(w):
                        b = wait_acc()
                        q0 = items[2 * w][1]
                        fn(T[:, q0:q0 + 256], acc[b][:, 0:256], ACT.Ln, scale=1.0 / P, bias=EC[:, 0:1], sem=f"acc_free{b}")
                        act.wait_ge(S(f"acc_free{b}"), c.pair("acc", -1)[1] + 2)
                        fn(T[:, q0:q0 + 256], T[:, q0:q0 + 256], ACT.Exp, scale=-0.5, sem="orr")

                    for i, (_, q, k0, blk) in enumerate(items):
                        slot = (2 * i + 1) % 4
                        nk = TOK if k0 == 0 else CTX
                        c.step("rl")
                        act.wait_ge(S("rl"), c.at("rl"))
                        fn(PR[:, slot, 0:nk], PR[:, slot, 0:nk], ACT.Copy, scale=RLN[:, i % 2:i % 2 + 1], sem="pb")
                        if i + 1 < len(items):
                            exp(2 * i + 2, items[i + 1][2])
                            exp(2 * i + 3, items[i + 1][2])
                        turned_hi(blk, i % 2, k0)
                        if (i % 2 == 0 and i) or i == len(items) - 1:
                            w = i // 2 - 1 if i % 2 == 0 else i // 2
                            if w:
                                sub(w - 1)
                            q0 = items[2 * w][1]
                            b = wait_acc()
                            settle()
                            fn(X[:, h + 4, q0:q0 + 256], acc[b][:, 0:256], ACT.Copy, sem="oraw")
                            fn(OSQ[:, w % 3, :], acc[b][:, 0:256], ACT.Square, sem=f"acc_free{b}")
                    sub(nb(l) - 1)
                act.wait_ge(S("od"), 4 * nb(0) * (l > 0) + 4 * nb(l))
                for k in range(KC):
                    fn(BR[:, 0, k, 0:n], X[:, k, 0:n], ACT.Copy, sem="bhi")
                for b in range(3):
                    if b == 0:
                        act.wait_ge(S("bsplit"), 8 * (l + 1))
                        for ch in range(CC):
                            fn(XC(l, ch), U[:, 0:conv_width(l)], ACT.Identity, scale=EC[:, 2:3],
                               bias=V[:, V_BDW + CC * l + ch:V_BDW + CC * l + ch + 1], sem="cbias")
                    with c.repeat(act, KC, per_merge_act(l, b)) as j:
                        mods = mod_here(l, b=b)
                        if mods:
                            hi()
                            hi(modt=1)
                        else:
                            hi(CC * P)
                        for i, (a, w) in enumerate(slim):
                            bb, m = c.pair("acc", -1 if l else -2)
                            act.wait_ge(S(f"acc_free{bb}"), m + 2)
                            b_ = wait_acc()
                            settle()
                            fn(G[:, a:a + w], acc[b_][:, 0:w], ACT.Sigmoid,
                               bias=V[:, bass.ds(j + (V_BGATE + 24 * l + 8 * b), 1)], sem=f"acc_free{b_}")
                            if mods and i == 0:
                                hi(CC * P, acc=nr(l) - 1, modt=1)
                        if mods:
                            hi(modt=2)
                            mod_row()
                        else:
                            hi()
                        c.step("acc", nr(l))
                    if b == 1:
                        w0 = conv_width(l)
                        exp_set()
                        c.step("acc", 2)
                        for ch in range(CC):
                            c.step("lcen")
                            act.wait_ge(S("lcen"), c.at("lcen"))
                            fn(US(l, ch), XC(l, ch), ACT.Square, sem="lsq")
                        for a, w in conv_halves(l):
                            b_ = wait_acc()
                            fn(U[:, UW + a:UW + a + w], acc[b_][:, 0:w], ACT.Ln, scale=1.0 / CONV_CH, bias=EC[:, 0:1], sem=f"acc_free{b_}")
                            act.wait_ge(S(f"acc_free{b_}"), c.pair("acc", -1)[1] + 2)
                        fn(U[:, UW:UW + w0], U[:, UW:UW + w0], ACT.Exp, scale=-0.5, sem="lrs")
                        for ch in range(CC):
                            o = CC * l + ch
                            c.step("lnx")
                            act.wait_ge(S("lnx"), c.at("lnx"))
                            fn(XC(l, ch), XC(l, ch), ACT.Silu, scale=V[:, V_GLN + o:V_GLN + o + 1], bias=V[:, V_BLN + o:V_BLN + o + 1], sem="lsw")
                            c.step("lsw")
                            act.wait_ge(S("lsw"), c.at("lsw"))
                            for s, o, m in conv_pieces(0, n):
                                fn(BR[:, 0, ch, s:s + m], X1[:, ch * XW + o:ch * XW + o + m], ACT.Copy, sem="chi")
                c.step("mdone", 1)
                act.wait_ge(S("mdone"), c.at("mdone"))
                for k in range(KC):
                    fn(H[:, 0, k, 0:n], MM[:, k, 0:n], ACT.Copy, sem="mhi")
                with c.repeat(act, 4, per_out(l)):
                    for s in range(2):
                        hi()
                        c.step("acc", nr(l))
                c.step("xres", 1)
                act.wait_ge(S("xres"), c.at("xres"))
                norm(l, 1, n)
                for g, (k0, m) in enumerate(GROUPS):
                    with c.repeat(act, m, dict(per_ffn(l, g), modt=2 * mod_here(l, g=g))) as f:
                        mods = mod_here(l, g=g)
                        hi()
                        if mods:
                            hi(modt=1)
                        for i, (a, w) in enumerate(slim):
                            bb, m_ = c.pair("acc", -1 if l else -2)
                            act.wait_ge(S(f"acc_free{bb}"), m_ + 2)
                            b_ = wait_acc()
                            fn(G[:, a:a + w], acc[b_][:, 0:w], ACT.Silu, sem=f"acc_free{b_}")
                            if mods and i == 0:
                                hi(acc=nr(l) - 1, modt=1)
                        if mods:
                            hi(modt=2)
                            mod_row()
                        else:
                            hi()
                        for i, (a, w) in enumerate(slim):
                            c.step("acc")
                            wait_read(act, c, "acc", 1)
                            settle()
                            fn(BR[:, 0, f, a:a + w], T[:, a:a + w], ACT.Copy, sem="midh")
                    last = l == DEPTH - 1 and g == len(GROUPS) - 1
                    with c.repeat(act, 3 if last else 4, per_out(l)):
                        for s in range(2):
                            hi()
                            c.step("acc", nr(l))
                    if last:
                        hi()

        @block.vector
        def _(dve):
            c = Counts()

            def wait_acc():
                b, n = c.pair("acc")
                dve.wait_ge(S("acc_full"), c.at("acc") + 2)
                c.step("acc")
                return b

            def own(name, ins, k=1):
                ins.then_inc(S(name), 1)
                c.step(name)
                dve.wait_ge(S(name), c.at(name))

            def tt(dst, a, b, op):
                return nc.vector.tensor_tensor(dst, a, b, op)

            def heads(p, n, nrs, is_q):
                c.step("acc", nrs)
                wait_read(dve, c, "acc", *range(1, nrs + 1))
                dve.sem_inc(S("dve_turn"), 1)
                own("rope", nc.vector.stream_shuffle(G[:, 0:LAT], XG[:, p, 0:LAT], [(k + 16) % 32 for k in range(32)]))
                tt(G[:, 0:LAT], G[:, 0:LAT], SIN, ALU.mult).then_inc(S("rope"), 1)
                tt(XG[:, p, 0:LAT], XG[:, p, 0:LAT], COS, ALU.mult).then_inc(S("rope"), 1)
                c.step("rope", 2)
                dve.wait_ge(S("rope"), c.at("rope"))
                tt(XG[:, p, 0:LAT], XG[:, p, 0:LAT], G[:, 0:LAT], ALU.add).then_inc(S("rope2"), 1)
                c.step("rope2")
                dve.wait_ge(S("rope2"), c.at("rope2"))
                c.step("rs")
                dve.wait_ge(S("rs"), c.at("rs"))
                tt(XG[:, p, 0:n], XG[:, p, 0:n], R[:, 0:n], ALU.mult).then_inc(S("y"), 1)
                c.step("y")
                dve.wait_ge(S("y"), c.at("y"))
                c.step("qhi")
                dve.wait_ge(S("qhi"), c.at("qhi"))
                w = 0 if is_q else 1
                tt(QK[:, w, 1, 0:n], XG[:, p, 0:n], QK[:, w, 0, 0:n].bitcast(F32), ALU.subtract).then_inc(S("qk"), 1)
                c.step("qk")

            def values():
                for a in range(2):
                    b, n = c.pair("aux")
                    c.step("aux")
                    c.step("vhi")
                    dve.wait_ge(S("vhi"), c.at("vhi"))
                    tt(VT[:, 1, 3 * a:3 * a + 3, :], v4(aux[b], 0, 3, P), VT[:, 0, 3 * a:3 * a + 3, :].bitcast(F32),
                       ALU.subtract).then_inc(S(f"aux_free{b}"), 1)

            def maximum(k, k0):
                s, _ = c.pair("sc")
                n = TOK if k0 == 0 else CTX
                dve.wait_ge(S("scored"), c.at("sc") + 1)
                nc.vector.tensor_reduce(NM[:, k % 4:k % 4 + 1], sco[s][:, 0:n], AX_X, ALU.max, negate=True).then_inc(S("max"), 1)
                c.step("sc")

            def turned_lo(blk, half, k0):
                for a in range(2 if k0 == 0 else 1):
                    b, n = c.pair("aux")
                    c.step("aux")
                    c.step("pth")
                    dve.wait_ge(S("pth"), c.at("pth"))
                    kk = slice(3 * a, 3 * a + 3) if k0 == 0 else slice(4, 6)
                    m = 3 if k0 == 0 else 2
                    q = slice(half * P, half * P + P)
                    tt(PT[:, blk % 2, 1, kk, q], v4(aux[b], 0, m, P), PT[:, blk % 2, 0, kk, q].bitcast(F32),
                       ALU.subtract).then_inc(S(f"aux_free{b}"), 1)

            def mod_group(g):
                c.step("mod")
                dve.wait_ge(S("mod_turned"), c.at("mod") + 1)
                dst = MOD1[:, bass.ds(g * 4, 4)].rearrange("p (k s) -> p k s", s=2)
                src = v4(sco[1], 0, 2, 4)
                bias = V[:, bass.ds(g * 4 + V_BMOD, 4)].rearrange("p (k s) -> p k s", s=2)
                tt(dst, src[:, :, 0:2], bias, ALU.add).then_inc(S("mod_part"), 1)
                dve.wait_ge(S("mod_part"), c.at("mod"))
                tt(dst, src[:, :, 2:4], dst, ALU.add).then_inc(S("mod_sum"), 1)

            def norm(l, k, n):
                dve.wait_ge(S("mod_sum"), c.at("mod") + 1)
                nc.vector.scalar_tensor_tensor(
                    A[:, l, k, :, :], MOD[:, l, SC1 if k == 0 else SC2, :, :], 1.0,
                    v4(V, V_G + (2 * l + k) * KC * 2, KC, 2), ALU.add, ALU.mult).then_inc(S("mod_gain"), 1)
                c.step("acc", 2)
                if (l, k) != (0, 0):
                    for j in range(1, KC):
                        dve.wait_ge(S("nsq"), c.at("nsq", j + 1))
                        own("nadd", tt(MM[:, 0, 0:n], MM[:, 0, 0:n], MM[:, j, 0:n], ALU.add))
                    c.step("nsq", KC)
                c.step("nrs")
                dve.wait_ge(S("nrs"), c.at("nrs"))

                def lo(j):
                    c.step("nhi")
                    dve.wait_ge(S("nhi"), c.at("nhi"))
                    tt(H[:, 1, j, 0:n], MM[:, j, 0:n], H[:, 0, j, 0:n].bitcast(F32), ALU.subtract).then_inc(S("h_ready"), 1)

                for j in range(KC):
                    tt(MM[:, j, 0:n], X[:, j, 0:n], R[:, 0:n], ALU.mult).then_inc(S("ntm"), 1)
                    if j >= 2:
                        lo(j - 2)
                lo(KC - 2)
                lo(KC - 1)

            def residual(l, j, rngs, part, final=None):
                for a, w in rngs:
                    b = wait_acc()
                    ps_ = stream_pieces(a, w)
                    for k, (s, m, st) in enumerate(ps_):
                        nc.vector.scalar_tensor_tensor(
                            X[:, j, s:s + m], acc[b][:, s - a:s - a + m], MOD[:, l, part, j, st:st + 1],
                            X[:, j, s:s + m], ALU.mult, ALU.add).then_inc(S(f"acc_free{b}" if k == len(ps_) - 1 else "xpart"), 1)

            def all_evacuated():
                for back in (1, 2):
                    b, n = c.pair("acc", -back)
                    dve.wait_ge(S(f"acc_free{b}"), n + 2)

            for name in ("madd", "glu", "mod_sum", "mid_chunks", "mid_half"):
                dve.sem_inc(S(name), 1)
            dve.wait_ge(S("vecs"), 16)
            dve.wait_ge(S("consts"), 16)
            dve.wait_ge(S("wdw"), 16)
            dve.wait_ge(S("wdw_zero"), 1)
            dve.wait_ge(S("u_zero"), 1)
            dve.wait_ge(S("scx_hi"), 1)
            tt(SCX[:, :, 2:4], SC[:, :, :], SCX[:, :, 0:2].bitcast(F32), ALU.subtract).then_inc(S("scx"), 1)
            for l in range(DEPTH):
                for m in range(2):
                    o = V_LAM + (l * 4 + m * 2) * HEAD
                    tt(G[:, (2 * l + m) * HEAD:(2 * l + m + 1) * HEAD], V[:, o:o + HEAD], V[:, o + HEAD:o + 2 * HEAD], ALU.mult).then_inc(S("lam_mul"), 1)
            dve.wait_ge(S("lam_mul"), 4)
            for i in range(4):
                nc.vector.tensor_reduce(LM[:, i:i + 1], G[:, i * HEAD:(i + 1) * HEAD], AX_X, ALU.add).then_inc(S("lam"), 1)
            dve.wait_ge(S("lam_exp"), 1)
            for l in range(DEPTH):
                init = 0.8 - 0.6 * math.exp(-0.3 * l)
                tt(LM[:, 12 + l:13 + l], LM[:, 9 + 2 * l:10 + 2 * l], LM[:, 8 + 2 * l:9 + 2 * l], ALU.subtract).then_inc(S("lam_sub"), 1)
                dve.wait_ge(S("lam_sub"), l + 1)
                nc.vector.tensor_scalar(NEGLAM[:, l:l + 1], LM[:, 12 + l:13 + l], -init, None, ALU.add).then_inc(S("lam_neg"), 1)
                nc.vector.tensor_scalar(GS[:, l:l + 1], V[:, V_GSUB + l:V_GSUB + l + 1], 1.0 - init, None, ALU.mult).then_inc(S("lam_neg"), 1)
            dve.wait_ge(S("lam_neg"), 4)
            dve.wait_ge(S("t_zero"), 1)
            with c.repeat(dve, MOD_FIRST, dict(mod=1, nsq=1, nadd=1)) as i:
                c.step("nsq")
                dve.wait_ge(S("nsq"), c.at("nsq"))
                own("nadd", tt(T[:, :], T[:, :], MM[:, i, :], ALU.add))
                mod_group(i)

            for l in range(DEPTH):
                wide, slim = ranges(l, True), ranges(l, False)
                n = n_tok(l)
                norm(l, 0, TOK)
                c.step("aux", 2)
                heads(1, TOK, 2, False)
                c.step("acc", 2)
                values()
                with c.repeat(dve, 4, per_gqa(l)) as j:
                    c.step("aux", 2)
                    heads(0, n, nr(l), True)
                    c.step("acc", nr(l) + 2 * nb(l))
                    items = [(hp, q, k0, hp * nb(l) + m) for hp in range(2) for q, k0, m in qtiles(l)]
                    maximum(0, items[0][2])
                    maximum(1, items[1][2])
                    for i, (hp, q, k0, blk) in enumerate(items):
                        nk = TOK if k0 == 0 else CTX
                        s = i % 4
                        ahead = min(2, len(items) - i)
                        dve.wait_ge(S("exp"), c.at("sc", 3 - ahead))
                        own("recip", nc.vector.reciprocal(RL[:, s:s + 1], L[:, s:s + 1]))
                        nc.vector.tensor_scalar(PR[:, s, 0:nk], PR[:, s, 0:nk], RL[:, s:s + 1], None, ALU.mult).then_inc(S("pn"), 1)
                        c.step("pn")
                        if i + 2 < len(items):
                            maximum(i + 2, items[i + 2][2])
                        turned_lo(blk, i % 2, k0)
                with c.repeat(dve, 4, per_diff(l)) as h:
                    acc0 = c.n["acc"]
                    c.step("aux", 2)
                    heads(0, n, nr(l), True)
                    c.step("aux", 2)
                    heads(1, TOK, 2, False)
                    c.step("acc", 2)
                    values()
                    for i, (a, w) in enumerate(slim):
                        c.step("acc")
                        wait_read(dve, c, "acc", 1)
                        for s, o, m in conv_pieces(a, w):
                            u = U[:, bass.ds(h * UW + (PAD + o), m)]
                            tt(u, u, XS[:, 1, s:s + m], ALU.mult).then_inc(S("glu"), 1)
                            c.step("glu")
                    items = [(0, q, k0, m) for q, k0, m in qtiles(l)]
                    for k in range(2):
                        maximum(k, items[0][2])

                    def sub(w):
                        q0 = items[2 * w][1]
                        c.step("orr")
                        dve.wait_ge(S("orr"), c.at("orr"))
                        o = X[:, h + 4, q0:q0 + 256]
                        nc.vector.scalar_tensor_tensor(o, o, GS[:, l:l + 1], T[:, q0:q0 + 256], ALU.mult, ALU.mult).then_inc(S("od"), 1)

                    for i, (_, q, k0, blk) in enumerate(items):
                        nk = TOK if k0 == 0 else CTX
                        s = (2 * i) % 4
                        dve.wait_ge(S("exp"), c.at("sc", 2))
                        own("recip", nc.vector.reciprocal(RL[:, s:s + 2], L[:, s:s + 2]))
                        tt(RLN[:, i % 2:i % 2 + 1], RL[:, s + 1:s + 2], NEGLAM[:, l:l + 1], ALU.mult).then_inc(S("rl"), 1)
                        if i + 1 < len(items):
                            maximum(2 * i + 2, items[i + 1][2])
                            maximum(2 * i + 3, items[i + 1][2])
                        c.step("pb")
                        dve.wait_ge(S("pb"), c.at("pb"))
                        nc.vector.scalar_tensor_tensor(PR[:, s, 0:nk], PR[:, s, 0:nk], RL[:, s:s + 1], PR[:, s + 1, 0:nk],
                                                       ALU.mult, ALU.add).then_inc(S("pn"), 1)
                        c.step("pn")
                        turned_lo(blk, i % 2, k0)
                        if (i % 2 == 0 and i) or i == len(items) - 1:
                            w = i // 2 - 1 if i % 2 == 0 else i // 2
                            if w:
                                sub(w - 1)
                    sub(nb(l) - 1)
                    c.n["acc"] = acc0 + per_diff(l)["acc"]
                for k in range(KC):
                    c.step("bhi")
                    dve.wait_ge(S("bhi"), c.at("bhi"))
                    tt(BR[:, 1, k, 0:n], X[:, k, 0:n], BR[:, 0, k, 0:n].bitcast(F32), ALU.subtract).then_inc(S("bsplit"), 1)

                def merge(b, j):
                    c.step("acc", nr(l))
                    for a, w in slim:
                        wait_read(dve, c, "acc", nr(l))
                        b_ = wait_acc()
                        if b == 0:
                            tt(MM[:, j, a:a + w], G[:, a:a + w], acc[b_][:, 0:w], ALU.mult).then_inc(S(f"acc_free{b_}"), 1)
                        else:
                            dve.wait_ge(S("madd"), c.at("madd") + 1)
                            tt(T[:, a:a + w], G[:, a:a + w], acc[b_][:, 0:w], ALU.mult).then_inc(S(f"acc_free{b_}"), 1)
                            dve.wait_ge(S(f"acc_free{b_}"), c.pair("acc", -1)[1] + 2)
                            tt(MM[:, j, a:a + w], MM[:, j, a:a + w], T[:, a:a + w], ALU.add).then_inc(S("madd"), 1)
                            c.step("madd")

                c.step("cbias", CC)
                dve.wait_ge(S("cbias"), c.at("cbias"))
                w0 = conv_width(l)
                for b in range(2):
                    pr = dict(per_merge(l, b), madd=nr(l) if b else 0, tap=TAPS4)
                    with c.repeat(dve, 2, {k: 4 * v for k, v in pr.items()}) as c2:
                        with c.repeat(dve, 4, pr) as q:
                            for t in range(TAPS4):
                                o = X1[:, bass.ds((c2 + 2 * b) * XW, w0)]
                                u = U[:, bass.ds((c2 + 2 * b) * UW + q * TAPS4 + t, w0)]
                                wt = WDW[:, l, :, :].rearrange("p c t -> p (c t)")[:, bass.ds((c2 + 2 * b) * 32 + q * TAPS4 + t, 1)]
                                own("tap", nc.vector.scalar_tensor_tensor(o, u, wt, o, ALU.mult, ALU.add))
                            if mod_here(l, b=b):
                                mod_group(c2 * 4 + q + (MOD_FIRST + b * KC))
                            merge(b, c2 * 4 + q)
                sum_ = U[:, 0:w0]
                tt(sum_, XC(l, 0), XC(l, 1), ALU.add).then_inc(S("lad"), 1)
                c.step("lad")
                for ch in (2, 3):
                    dve.wait_ge(S("lad"), c.at("lad"))
                    tt(sum_, sum_, XC(l, ch), ALU.add).then_inc(S("lad" if ch == 2 else "lsum"), 1)
                    if ch == 2:
                        c.step("lad")
                for i, (a, w) in enumerate(conv_halves(l)):
                    b_ = wait_acc()
                    for ch in range(CC):
                        o = X1[:, ch * XW + a:ch * XW + a + w]
                        ins = nc.vector.scalar_tensor_tensor(o, acc[b_][:, 0:w], -1.0 / CONV_CH, o, ALU.mult, ALU.add)
                        ins.then_inc(S(f"acc_free{b_}") if ch == CC - 1 else S("lc0"), 1)
                    dve.wait_ge(S(f"acc_free{b_}"), c.pair("acc", -1)[1] + 2)
                for ch in range(CC):
                    dve.sem_inc(S("lcen"), 1)
                c.step("acc", 2)
                for ch in range(1, CC):
                    dve.wait_ge(S("lsq"), CC * l + ch + 1)
                    ins = tt(US(l, 0), US(l, 0), US(l, ch), ALU.add)
                    if ch < CC - 1:
                        own("lad", ins)
                    else:
                        ins.then_inc(S("lsum"), 1)
                dve.wait_ge(S("lrs"), l + 1)
                for ch in range(CC):
                    tt(XC(l, ch), XC(l, ch), U[:, UW:UW + w0], ALU.mult).then_inc(S("lnx"), 1)
                for ch in range(CC):
                    for s, o, m in conv_pieces(0, n):
                        c.step("chi")
                        dve.wait_ge(S("chi"), c.at("chi"))
                        last = s + m == n
                        tt(BR[:, 1, ch, s:s + m], X1[:, ch * XW + o:ch * XW + o + m],
                           BR[:, 0, ch, s:s + m].bitcast(F32), ALU.subtract).then_inc(S("c_split" if last else "clo"), 1)
                if l == 0:
                    dve.wait_ge(S("c_split"), CC * (l + 1))
                    nc.vector.memset(U[:, :], 0.0).then_inc(S("u_zero"), 1)
                with c.repeat(dve, KC, dict(per_merge(l, 2), madd=nr(l))) as j:
                    if mod_here(l, b=2):
                        mod_group(j + (MOD_FIRST + 2 * KC))
                    merge(2, j)
                dve.wait_ge(S("madd"), c.at("madd") + 1)
                dve.sem_inc(S("mdone"), 1)
                for k in range(KC):
                    c.step("mhi")
                    dve.wait_ge(S("mhi"), c.at("mhi"))
                    tt(H[:, 1, k, 0:n], MM[:, k, 0:n], H[:, 0, k, 0:n].bitcast(F32), ALU.subtract).then_inc(S("msplit"), 1)
                dve.wait_ge(S("x"), 16 * (l + 2))
                with c.repeat(dve, 4, per_out(l)) as j:
                    for s in range(2):
                        residual(l, j * 2 + s, slim, GT1)
                all_evacuated()
                dve.sem_inc(S("xres"), 1)
                norm(l, 1, n)
                for g, (k0, m) in enumerate(GROUPS):
                    with c.repeat(dve, m, per_ffn(l, g)) as f:
                        if mod_here(l, g=g):
                            mod_group(f + (MOD_GROUPS + (g + 1) * KC))
                        c.step("acc", nr(l))
                        for i, (a, w) in enumerate(slim):
                            wait_read(dve, c, "acc", nr(l))
                            b_ = wait_acc()
                            name = "mid_chunks" if i == len(slim) - 1 else "mid_half"
                            dve.wait_ge(S(name), c.at(name) + 1)
                            tt(T[:, a:a + w], G[:, a:a + w], acc[b_][:, 0:w], ALU.mult).then_inc(S(f"acc_free{b_}"), 1)
                            c.step("midh")
                            dve.wait_ge(S("midh"), c.at("midh"))
                            ins = tt(BR[:, 1, f, a:a + w], T[:, a:a + w], BR[:, 0, f, a:a + w].bitcast(F32), ALU.subtract)
                            ins.then_inc(S(name), 1)
                            c.step(name)
                    with c.repeat(dve, 4, per_out(l)) as j:
                        for s in range(2):
                            residual(l, j * 2 + s, slim, GT2)
                    all_evacuated()
                dve.sem_inc(S("x_done"), 1)


def kernel(**inputs):
    import concourse.bacc as _bacc
    from concourse.bass_utils import run_bass_kernel_spmd as _run

    a = {k: np.asarray(v) for k, v in inputs.items()}
    f32 = np.float32

    def chunks(v):
        return np.moveaxis(v.reshape(v.shape[:-1] + (-1, P)), -1, 0)

    def tiles(w):
        l, k, n = w.shape
        return np.ascontiguousarray(w.reshape(l, k // P, P, n // P, P).transpose(0, 3, 2, 1, 4).reshape(l, n // P, P, k))

    cols = lambda o: list(range(o, o + P))
    order = cols(512) + cols(640)
    for j in range(4):
        order += list(range(64 * j, 64 * j + 64)) + list(range(256 + 64 * j, 256 + 64 * j + 64)) + cols(2304 + P * j)
    for h in range(4):
        order += cols(768 + P * h) + cols(1280 + P * h) + cols(1792 + P * h) + cols(2816 + P * h)
    rows_a = [r for j in range(4) for o in (64 * j, 256 + 64 * j) for r in range(o, o + 64)]
    w_in = tiles(a["w_in"][:, :, order])
    w_br = np.concatenate([tiles(a["w_a"][:, rows_a, :]), tiles(a["w_b"]), tiles(a["w_c"])], axis=1)
    fi = tiles(a["w_ffn_in"])
    w_fi = np.ascontiguousarray(np.stack([fi[:, :FC], fi[:, FC:]], axis=2).reshape(DEPTH, 2 * FC, P, D))
    w_mod = np.ascontiguousarray(a["w_mod"].reshape(DEPTH, 2, 4, P, MOD_GROUPS, MOD_GROUP).transpose(0, 4, 1, 3, 2, 5)
                                 .reshape(DEPTH * MOD_GROUPS, 2, P, D))

    x_all = np.concatenate([a["x"][0], a["ctx"][0]], axis=0)
    xT = np.ascontiguousarray(x_all.T.reshape(KC, P, TOK).transpose(1, 0, 2))

    two = lambda v: np.repeat(v[..., None], 2, axis=-1).reshape(P, -1)
    heads2 = lambda v: np.concatenate([v, v], axis=-1)
    gains = np.stack([heads2(a[k]) for k in ("g_q_gqa", "g_k_gqa", "g_q_diff", "g_k_diff")], axis=1)
    lam = np.stack([a[k] for k in ("lambda_q1", "lambda_k1", "lambda_q2", "lambda_k2")], axis=1)
    vecs = np.concatenate([
        np.stack([chunks(a["c"][0]), chunks(a["c_ctx"])], axis=-1).reshape(P, -1),
        two(chunks(a["b_mod"])),
        two(chunks(np.stack([a["g_norm1"], a["g_norm2"]], axis=1))),
        chunks(a["b_gate"]).reshape(P, -1),
        gains.transpose(2, 0, 1).reshape(P, -1),
        a["g_subln"].T,
        chunks(a["b_dw"]).reshape(P, -1),
        chunks(a["g_conv_ln"]).reshape(P, -1),
        chunks(a["b_conv_ln"]).reshape(P, -1),
        np.broadcast_to(lam.reshape(1, -1), (P, lam.size)),
    ], axis=1)
    wdw = np.ascontiguousarray(a["w_dw"].reshape(DEPTH, TAPS, CC, P).transpose(3, 0, 2, 1))

    row = np.repeat(np.arange(LAT // GRID_W, dtype=f32), GRID_W)
    col = np.tile(np.arange(GRID_W, dtype=f32), LAT // GRID_W)
    inv = (f32(THETA) ** (-np.arange(16, dtype=f32) / f32(16))).astype(f32)
    feature = np.arange(P) % HEAD
    ang = np.where((feature < 32)[:, None], row[None, :], col[None, :]).astype(f32) * inv[feature % 16][:, None]
    sign = np.where(feature % 32 < 16, -1.0, 1.0).astype(f32)[:, None]
    same = np.arange(P)[:, None] // HEAD == np.arange(P)[None, :] // HEAD
    consts = np.concatenate([np.cos(ang), np.sin(ang) * sign, np.ones((P, P)), same, np.eye(P)], axis=1).astype(f32)

    nc = _bacc.Bacc("TRN2", target_bir_lowering=False, num_devices=1)
    arrays = {"xT": xT, "vecs": np.ascontiguousarray(vecs), "consts": consts, "wdw": wdw, "w_mod": w_mod, "w_in": w_in,
              "w_gate": tiles(a["w_gate"]), "w_br": np.ascontiguousarray(w_br), "w_out": tiles(a["w_out"]),
              "w_fi": w_fi, "w_fo": tiles(a["w_ffn_out"])}
    ins = {k: nc.dram_tensor("in_" + k, v.shape, F32, kind="ExternalInput").ap() for k, v in arrays.items()}
    out = nc.dram_tensor("out_x", (P, KC, LAT), F32, kind="ExternalOutput").ap()
    build(nc, out=out, **ins)
    r = _run(nc, [{"in_" + k: v for k, v in arrays.items()}], core_ids=[0])
    y = r.results[0]["out_x"]
    return np.ascontiguousarray(y.transpose(1, 0, 2).reshape(D, LAT).T).reshape(1, LAT, D)
```
